# Optimizing a Trainium2 kernel written in Bass

```python
import jax, jax.numpy as jnp
from jax import lax
import numpy as np

D_MODEL = 2048
BATCH = 1
SEQ = 256
DEPTH = 1

CHUNK = 64
EPS = 1e-6

ATTN_HEADS = 16
ATTN_KV_HEADS = 2
ATTN_HEAD_DIM = 64
ATTN_GROUP = ATTN_HEADS // ATTN_KV_HEADS
ATTN_WIDTH = ATTN_HEADS * ATTN_HEAD_DIM
ATTN_KV_WIDTH = ATTN_KV_HEADS * ATTN_HEAD_DIM
WINDOW = 128
WINDOW_CHUNKS = WINDOW // CHUNK

HG_WIDTH = D_MODEL - ATTN_WIDTH
HG_EXPAND = 128
HG_HEADS = HG_WIDTH // HG_EXPAND
HG_KEY_DIM = HG_EXPAND
HG_VAL_DIM = HG_WIDTH // HG_HEADS
HG_KEY_WIDTH = HG_HEADS * HG_KEY_DIM

D_MIX = ATTN_WIDTH + HG_WIDTH

D_FF = 5632
CONV_WIDTH = 3

SPLIT_SIZES = (ATTN_WIDTH, ATTN_KV_WIDTH, ATTN_KV_WIDTH, HG_KEY_WIDTH, HG_KEY_WIDTH, HG_WIDTH, HG_WIDTH)
SPLIT_POINTS = tuple(int(s) for s in np.cumsum(SPLIT_SIZES)[:-1])
D_IN_PROJ = int(sum(SPLIT_SIZES))

kernel_name = "hybrid_swa_hgrn2_convffn"

def rms_norm(x, gain):
    xf = x.astype(jnp.float32)
    y = xf * lax.rsqrt(jnp.mean(xf * xf, axis=-1, keepdims=True) + EPS)
    return (y * gain.astype(jnp.float32)).astype(x.dtype)

def alibi_slopes(n_heads):
    return jnp.asarray(np.array([2.0 ** (-8.0 * (h + 1) / n_heads) for h in range(n_heads)], dtype=np.float32))

def sliding_window_attention(q, k, v, q_gain, k_gain, sinks):
    B, S = q.shape[0], q.shape[1]
    nc = S // CHUNK
    qc = rms_norm(q.reshape(B, nc, CHUNK, ATTN_KV_HEADS, ATTN_GROUP, ATTN_HEAD_DIM), q_gain)
    kc = rms_norm(k.reshape(B, nc, CHUNK, ATTN_KV_HEADS, ATTN_HEAD_DIM), k_gain)
    vc = v.reshape(B, nc, CHUNK, ATTN_KV_HEADS, ATTN_HEAD_DIM)

    def band(t):
        tp = jnp.pad(t, ((0, 0), (WINDOW_CHUNKS - 1, 0), (0, 0), (0, 0), (0, 0)))
        return jnp.concatenate([tp[:, j:j + nc] for j in range(WINDOW_CHUNKS)], axis=2)

    kb, vb = band(kc), band(vc)
    scores = jnp.einsum('bnqhgd,bnkhd->bnhgqk', qc, kb).astype(jnp.float32) * (ATTN_HEAD_DIM ** -0.5)

    chunk_idx = jnp.arange(nc)
    q_pos = chunk_idx[:, None] * CHUNK + jnp.arange(CHUNK)[None, :]
    k_pos = (chunk_idx[:, None] - (WINDOW_CHUNKS - 1)) * CHUNK + jnp.arange(WINDOW)[None, :]
    dist = jnp.abs(q_pos[:, :, None] - k_pos[:, None, :]).astype(jnp.float32)
    valid = k_pos >= 0

    slopes = alibi_slopes(ATTN_HEADS).reshape(ATTN_KV_HEADS, ATTN_GROUP)
    scores = scores - slopes[None, None, :, :, None, None] * dist[None, :, None, None, :, :]
    scores = jnp.where(valid[None, :, None, None, None, :], scores, -1e30)

    sink = jnp.broadcast_to(sinks.astype(jnp.float32).reshape(1, 1, ATTN_KV_HEADS, ATTN_GROUP, 1, 1),
                            scores.shape[:-1] + (1,))
    probs = jax.nn.softmax(jnp.concatenate([scores, sink], axis=-1), axis=-1)[..., :-1]
    out = jnp.einsum('bnhgqk,bnkhd->bnqhgd', probs.astype(vb.dtype), vb)
    return out.reshape(B, S, ATTN_WIDTH)

def hgrn2(q, f, i, g, lower_bound, norm_gain):
    B, S = q.shape[0], q.shape[1]
    nc = S // CHUNK
    out_dtype = q.dtype
    qf = jax.nn.silu(q.astype(jnp.float32))
    forget = lower_bound + (1.0 - lower_bound) * jax.nn.sigmoid(f.astype(jnp.float32))
    kf = 1.0 - forget
    log_f = jnp.log(forget)

    def to_chunks(t, d):
        return t.reshape(B, nc, CHUNK, HG_HEADS, d).transpose(1, 0, 3, 2, 4)

    xs = (to_chunks(qf, HG_KEY_DIM), to_chunks(kf, HG_KEY_DIM),
          to_chunks(log_f, HG_KEY_DIM), to_chunks(i.astype(jnp.float32), HG_VAL_DIM))
    causal = jnp.tril(jnp.ones((CHUNK, CHUNK), dtype=bool))

    def step(state, inp):
        q_c, k_c, lf_c, v_c = inp
        b = jnp.cumsum(lf_c, axis=-2)
        rel = b[..., :, None, :] - b[..., None, :, :]
        decay = jnp.exp(jnp.where(causal[:, :, None], rel, -jnp.inf))
        scores = jnp.einsum('bhtd,bhsd,bhtsd->bhts', q_c, k_c, decay)
        intra = jnp.einsum('bhts,bhsv->bhtv', scores, v_c)
        inter = jnp.einsum('bhtd,bhdv->bhtv', q_c * jnp.exp(b), state)
        b_last = b[..., -1:, :]
        new_state = (jnp.exp(b_last)[..., 0, :, None] * state
                     + jnp.einsum('bhsd,bhsv->bhdv', k_c * jnp.exp(b_last - b), v_c))
        return new_state, intra + inter

    state0 = jnp.zeros((B, HG_HEADS, HG_KEY_DIM, HG_VAL_DIM), jnp.float32)
    _, ys = lax.scan(step, state0, xs)
    o = ys.transpose(1, 0, 3, 2, 4).reshape(B, S, HG_HEADS, HG_VAL_DIM)
    o = rms_norm(o, norm_gain)
    o = o * jax.nn.silu(g.astype(jnp.float32)).reshape(B, S, HG_HEADS, HG_VAL_DIM)
    return o.reshape(B, S, HG_WIDTH).astype(out_dtype)

def conv_ffn(h, w_up, conv_w, conv_b, w_down):
    S = h.shape[1]
    u = h @ w_up
    up = jnp.pad(u, ((0, 0), (CONV_WIDTH - 1, 0), (0, 0)))
    u = sum(conv_w[j] * up[:, j:j + S] for j in range(CONV_WIDTH)) + conv_b
    a, b = jnp.split(u, 2, axis=-1)
    return (jax.nn.silu(a) * b) @ w_down

def setup_inputs(seed: int = 0) -> dict:
    key = jax.random.key(seed)
    ks = jax.random.split(key, 16)
    nrm = jax.random.normal
    return {
        "x": nrm(ks[0], (BATCH, SEQ, D_MODEL), jnp.float32),
        "attn_norm": 1.0 + 0.02 * nrm(ks[1], (DEPTH, D_MODEL), jnp.float32),
        "w_in": nrm(ks[2], (DEPTH, D_MODEL, D_IN_PROJ), jnp.float32) * D_MODEL ** -0.5,
        "q_norm": 1.0 + 0.02 * nrm(ks[3], (DEPTH, ATTN_HEAD_DIM), jnp.float32),
        "k_norm": 1.0 + 0.02 * nrm(ks[4], (DEPTH, ATTN_HEAD_DIM), jnp.float32),
        "attn_sinks": 0.5 * nrm(ks[5], (DEPTH, ATTN_HEADS), jnp.float32),
        "hg_lb_logits": 0.5 * nrm(ks[6], (DEPTH + 1, HG_KEY_WIDTH), jnp.float32),
        "hg_norm": 1.0 + 0.02 * nrm(ks[7], (DEPTH, HG_VAL_DIM), jnp.float32),
        "w_out": nrm(ks[8], (DEPTH, D_MIX, D_MODEL), jnp.float32) * D_MIX ** -0.5,
        "ffn_norm": 1.0 + 0.02 * nrm(ks[9], (DEPTH, D_MODEL), jnp.float32),
        "w_ffn_up": nrm(ks[10], (DEPTH, D_MODEL, 2 * D_FF), jnp.float32) * D_MODEL ** -0.5,
        "ffn_conv_w": nrm(ks[11], (DEPTH, CONV_WIDTH, 2 * D_FF), jnp.float32) * CONV_WIDTH ** -0.5,
        "ffn_conv_b": 0.01 * nrm(ks[12], (DEPTH, 2 * D_FF), jnp.float32),
        "w_ffn_down": nrm(ks[13], (DEPTH, D_FF, D_MODEL), jnp.float32) * D_FF ** -0.5,
    }

def reference(x, attn_norm, w_in, q_norm, k_norm, attn_sinks, hg_lb_logits, hg_norm, w_out,
              ffn_norm, w_ffn_up, ffn_conv_w, ffn_conv_b, w_ffn_down):
    lower_bounds = jnp.cumsum(jax.nn.softmax(hg_lb_logits.astype(jnp.float32), axis=0), axis=0)
    for l in range(DEPTH):
        h = rms_norm(x, attn_norm[l])
        p = h @ w_in[l]
        aq, ak, av, hq, hf, hi, hg = jnp.split(p, SPLIT_POINTS, axis=-1)
        attn_out = sliding_window_attention(aq, ak, av, q_norm[l], k_norm[l], attn_sinks[l])
        hg_out = hgrn2(hq, hf, hi, hg, lower_bounds[l], hg_norm[l])
        mix = jnp.concatenate([attn_out, hg_out], axis=-1)
        x = x + mix @ w_out[l]
        h = rms_norm(x, ffn_norm[l])
        x = x + conv_ffn(h, w_ffn_up[l], ffn_conv_w[l], ffn_conv_b[l], w_ffn_down[l])
    return x


_drawn_inputs = setup_inputs


def setup_inputs(seed=0):
    import zlib

    import numpy as np

    out = dict(_drawn_inputs(seed))
    spreads = {}
    factors = {'attn_norm': 3.967,
     'q_norm': 8.0,
     'k_norm': 8.0,
     'attn_sinks': 8.0,
     'hg_norm': 6.236,
     'ffn_norm': 11.593,
     'ffn_conv_b': 24.499}
    for name, (base, spread) in spreads.items():
        noise = np.random.default_rng([zlib.crc32(name.encode()), seed]).standard_normal(out[name].shape)
        drawn = base * np.exp(spread * noise) if base else spread * noise
        out[name] = __import__('jax').numpy.asarray(drawn.astype(out[name].dtype))
    for name, factor in factors.items():
        out[name] = (out[name] * factor).astype(out[name].dtype)
    return out
```

```python
import concourse.bass as bass
from concourse import mybir
from contextlib import ExitStack

F32 = mybir.dt.float32
F32R = mybir.dt.float32r
I32 = mybir.dt.int32
ACT = mybir.ActivationFunctionType
ALU = mybir.AluOpType
AX = mybir.AxisListType.X

P = 128
D_MODEL, SEQ, CHUNK = 2048, 256, 64
EPS = 1e-6
HEADS, KV_HEADS, HEAD_DIM = 16, 2, 64
HG_HEADS, HG_DIM = 8, 128
D_FF, CONV = 5632, 3
KT = D_MODEL // P
KT_FF = D_FF // P
TT = SEQ // P
RING = 4
FREE = 1
BANK_PAIRS = 2
GC = 256
GT = 512
Q_GROUPS = HEADS * HEAD_DIM // GC
PAIRS = HG_HEADS // 2
COL_Q, COL_KV = 0, HEADS * HEAD_DIM
COL_HQ = COL_KV + 2 * KV_HEADS * HEAD_DIM
COL_HF = COL_HQ + HG_HEADS * HG_DIM
COL_HI = COL_HF + HG_HEADS * HG_DIM
COL_HG = COL_HI + HG_HEADS * HG_DIM
LEVELS = [1, 2, 4, 8, 16, 32, 64]
NL = len(LEVELS)
UP_GROUPS = D_FF // GC
OUT_GROUPS = D_MODEL // GT
G_F0 = 1 + Q_GROUPS
G_OUT = G_F0 + 4 * PAIRS
G_UP = G_OUT + OUT_GROUPS
G_DOWN = G_UP + 2 * UP_GROUPS
QUADS_OUT = KT // 8
Q_OUT = G_OUT
Q_UP = Q_OUT + QUADS_OUT * OUT_GROUPS
Q_DOWN = Q_UP + 2 * UP_GROUPS
DOWN_UNITS = KT_FF // 2
FAR = -1e34
SIG_MIN = -43.0
FORGET_MIN = 2.0 ** -63


def hybrid_layer(nc, x, attn_norm, w_in, q_norm, k_norm, sinks, lb_logits, hg_norm, w_out,
                 ffn_norm, w_up, conv_w, conv_b, w_down, out):
    ctx = ExitStack()
    with ctx:
        def sb(name, shape, dt=F32):
            return ctx.enter_context(nc.sbuf_tensor(name, shape, dt))

        def sem(name):
            return ctx.enter_context(nc.semaphore(name))

        xt = sb("xt", [P, TT, D_MODEL])
        hs = sb("hs", [P, KT, 2 * SEQ], F32R)
        raw = sb("raw", [P, RING, 1024])
        w_hi = sb("w_hi", [P, RING, 1024], F32R)
        w_lo = sb("w_lo", [P, RING, 1024], F32R)
        ident = sb("ident", [P, P])
        head_mean = sb("head_mean", [P, P])
        all_mean = sb("all_mean", [P, P])
        slopes = sb("slopes", [P, HEADS])
        sink = sb("sink", [P, HEADS])
        eps = sb("eps", [P, 1])
        rows = sb("rows", [P, 1 + 1 + CONV, P])
        N_SMALL = 2 * HG_HEADS + 3
        N_CONV = 2 * D_FF // P
        cols = sb("cols", [P, N_SMALL + (1 + CONV) * N_CONV])
        lb = sb("lb", [P, HG_HEADS])
        one_lb = sb("one_lb", [P, HG_HEADS])
        lb_t = sb("lb_t", [P, 4, HG_HEADS])
        q_gain = sb("q_gain", [P, 1])
        ss = sb("ss", [P, TT])
        K_GAIN = 2 * HG_HEADS + 1
        HG_GAIN = 2 * HG_HEADS + 2
        C_BIAS = N_SMALL

        def conv_col(tap):
            return N_SMALL + (1 + tap) * N_CONV

        def region(name, size):
            sb(name, [P, size // 4])
            return [nc.sbuf_base - size, nc.sbuf_base]

        def sb_at(place, name, shape, dt=F32):
            size = 4
            for n in shape[1:]:
                size *= n
            start = place[0]
            place[0] += size
            place[0] += -place[0] % 32
            assert place[0] <= place[1], name
            return nc.alloc_sbuf_tensor_at(name, shape, dt, offset=start)

        small = region("small_region", 8448)
        place = list(small)
        level_mask = sb_at(place, "level_mask", [P, NL + 1, P])
        tile_start = sb_at(place, "tile_start", [P, 2 * SEQ])
        dist = sb_at(place, "dist", [P, 3 * P])
        place = list(small)
        U = sb_at(place, "U", [P, 2, SEQ + 2])
        C = sb_at(place, "C", [P, 2, 2, SEQ])

        large = region("large_region", KT_FF * 2 * SEQ * 4)
        place = list(large)
        mix = sb_at(place, "mix", [P, KT, 2 * SEQ], F32R)
        FE = sb_at(place, "FE", [P, 2, SEQ])
        QE = sb_at(place, "QE", [P, 2, SEQ])
        GE = sb_at(place, "GE", [P, 2, SEQ])
        IE = sb_at(place, "IE", [P, 2, SEQ])
        V = sb_at(place, "V", [P, 2, TT, P])
        SG = sb_at(place, "SG", [P, 2 * SEQ])
        SQ = sb_at(place, "SQ", [P, 2 * SEQ])
        RS = sb_at(place, "RS", [P, 2 * SEQ])
        ST = sb_at(place, "ST", [P, 2, 3, P])
        shared = list(place)
        K = sb_at(place, "K", [P, 2, SEQ])
        LF = sb_at(place, "LF", [P, 2 * SEQ])
        B = sb_at(place, "B", [P, 2 * SEQ])
        XQ = sb_at(place, "XQ", [P, NL + 1, 2 * SEQ])
        XK = sb_at(place, "XK", [P, NL, 2 * SEQ])
        SM = sb("SM", [P, NL + 1, P])
        place = list(shared)
        kz = sb_at(place, "kz", [P, KV_HEADS * 2, SEQ])
        vt = sb_at(place, "vt", [P, TT, P])
        QN = sb_at(place, "QN", [P, 2, SEQ])
        PR = sb_at(place, "PR", [P, 2, 3 * P])
        PT = sb_at(place, "PT", [P, 3 * P])
        AO = sb_at(place, "AO", [P, TT, 4 * HEAD_DIM])
        top = sb_at(place, "top", [P, 4, TT])
        exp_sink = sb_at(place, "exp_sink", [P, TT, 4])
        den = sb_at(place, "den", [P, TT, 4])
        place = list(shared)
        gain = sb_at(place, "gain", [P, D_MODEL])
        hn = sb_at(place, "hn", [P, TT, D_MODEL])
        place = list(large)
        gated = sb_at(place, "gated", [P, KT_FF, 2 * SEQ], F32R)

        bank = [ctx.enter_context(nc.psum_tensor(f"bank{i}", [P, 512], F32)) for i in range(8)]

        loaded = [sem(f"loaded{i}") for i in range(RING)]
        units_hi = sem("units_hi")
        units_split = sem("units_split")
        units_used = sem("units_used")
        groups_evacuated = sem("groups_evacuated")
        x_loaded = [sem(f"x_loaded{t}") for t in range(TT)]
        gain_loaded, rows_loaded = sem("gain_loaded"), sem("rows_loaded")
        pool_done, masks_made, cols_made, params_made = (
            sem("pool_done"), sem("masks_made"), sem("cols_made"), sem("params_made"))
        setup_step, mask_step = sem("setup_step"), sem("mask_step")
        param_step, param_exp = sem("param_step"), sem("param_exp")
        rows_transposed, xk_cleared = sem("rows_transposed"), sem("xk_cleared")
        x_squared, x_rms, x_rs, x_normed = sem("x_squared"), sem("x_rms"), sem("x_rs"), sem("x_normed")
        x_transposed, h_hi, h_lo = sem("x_transposed"), sem("h_hi"), sem("h_lo")
        att_squared, att_mean, att_ln, att_rs, qk_normed = (
            sem("att_squared"), sem("att_mean"), sem("att_ln"), sem("att_rs"), sem("qk_normed"))
        kz_made, v_transposed, vt_made = sem("kz_made"), sem("v_transposed"), sem("vt_made")
        scores_made, biased, max_made, top_made = (
            sem("scores_made"), sem("biased"), sem("max_made"), sem("top_made"))
        exp_made, p_transposed, pt_made, pv_made = (
            sem("exp_made"), sem("p_transposed"), sem("pt_made"), sem("pv_made"))
        sink_made, den_summed, den_inverted, att_scaled = (
            sem("sink_made"), sem("den_summed"), sem("den_inverted"), sem("att_scaled"))
        att_transposed, att_hi, att_lo = sem("att_transposed"), sem("att_hi"), sem("att_lo")
        sg_clamped, sg_exp, sg_ln, sg_made = (
            sem("sg_clamped"), sem("sg_exp"), sem("sg_ln"), sem("sg_made"))
        forget_scaled, forget_made, log_made, k_made, sum_made = (
            sem("forget_scaled"), sem("forget_made"), sem("log_made"), sem("k_made"), sem("sum_made"))
        exponents_made, decays_made, k_scaled, silu_q, q_scaled, silu_g = (
            sem("exponents_made"), sem("decays_made"), sem("k_scaled"), sem("silu_q"),
            sem("q_scaled"), sem("silu_g"))
        i_transposed, v_made, levels_made, masked, st_made = (
            sem("i_transposed"), sem("v_made"), sem("levels_made"), sem("masked"), sem("st_made"))
        cross_made, cross_copied, o_made, o_squared, o_mean, o_ln, o_rs = (
            sem("cross_made"), sem("cross_copied"), sem("o_made"), sem("o_squared"),
            sem("o_mean"), sem("o_ln"), sem("o_rs"))
        o_normed, o_gated, hg_hi, hg_lo = sem("o_normed"), sem("o_gated"), sem("hg_hi"), sem("hg_lo")
        u_cleared, tap2, tap1, tap0 = sem("u_cleared"), sem("tap2"), sem("tap1"), sem("tap0")
        silu_a, ab_made, gated_hi, gated_lo = (
            sem("silu_a"), sem("ab_made"), sem("gated_hi"), sem("gated_lo"))
        stored = sem("stored")

        w_in_v = w_in.rearrange("(k p) n -> p k n", p=P)
        w_out_v = w_out.rearrange("(k p) n -> p k n", p=P)
        w_up_v = w_up.rearrange("(k p) n -> p k n", p=P)
        w_down_v = w_down.rearrange("(k p) n -> p k n", p=P)
        x_v = x.rearrange("(t p) n -> p t n", p=P)
        out_v = out.rearrange("(t p) n -> p t n", p=P)

        def pair_of(group):
            b = 2 * (group % BANK_PAIRS)
            return bank[b], bank[b + 1]

        def halves(ap, width):
            v = ap.rearrange("p (n two w) -> p n two w", two=2, w=width)
            return v[:, :, 0, :], v[:, :, 1, :]

        block = ctx.enter_context(nc.Block())

        @block.sync
        def _(sp):
            for t in range(TT):
                sp.dma_start(xt[:, t, :], x_v[:, t, :]).then_inc(x_loaded[t], 16)
                if t == 0:
                    sp.dma_start(gain[:, :], attn_norm.broadcast_to([P, D_MODEL])).then_inc(gain_loaded, 16)

            def load_unit(quad, i, view, row, rows_n, col, cols_n):
                sp.wait_ge(units_split, quad * RING + i + 1)
                sp.dma_start(raw[:, i, :].rearrange("p (k n) -> p k n", k=rows_n),
                             view[:, row:row + rows_n, bass.ds(col, cols_n)]).then_inc(loaded[i], 16)

            def load_channels(quad, view, col):
                for i in range(RING):
                    load_unit(quad, i, view, 4 * i, 4, col, GC)

            load_channels(0, w_in_v, COL_KV)
            with sp.Fori(0, Q_GROUPS) as g:
                load_channels(g + 1, w_in_v, g * GC + COL_Q)
            load_channels(G_F0, w_in_v, COL_HF)
            load_channels(G_F0 + 1, w_in_v, COL_HQ)
            with sp.Fori(0, PAIRS - 1) as j:
                load_channels(j * 4 + G_F0 + 2, w_in_v, j * GC + COL_HI)
                load_channels(j * 4 + G_F0 + 3, w_in_v, j * GC + COL_HG)
                load_channels(j * 4 + G_F0 + 4, w_in_v, j * GC + COL_HF + GC)
                load_channels(j * 4 + G_F0 + 5, w_in_v, j * GC + COL_HQ + GC)
            load_channels(G_OUT - 2, w_in_v, COL_HI + (PAIRS - 1) * GC)
            load_channels(G_OUT - 1, w_in_v, COL_HG + (PAIRS - 1) * GC)
            with sp.Fori(0, OUT_GROUPS) as n:
                for c in range(QUADS_OUT):
                    for i in range(RING):
                        load_unit(n * QUADS_OUT + Q_OUT + c, i, w_out_v, 8 * c + 2 * i, 2, n * GT, GT)
            sp.wait_ge(cross_made, PAIRS)
            sp.dma_start(gain[:, :], ffn_norm.broadcast_to([P, D_MODEL])).then_inc(gain_loaded, 16)
            with sp.Fori(0, UP_GROUPS) as g:
                load_channels(g * 2 + Q_UP, w_up_v, g * GC)
                load_channels(g * 2 + Q_UP + 1, w_up_v, g * GC + D_FF)
            with sp.Fori(0, OUT_GROUPS // 2) as m:
                for v in range(2 * DOWN_UNITS):
                    n, u = divmod(v, DOWN_UNITS)
                    load_unit(m * (2 * DOWN_UNITS // RING) + Q_DOWN + v // RING, v % RING,
                              w_down_v, 2 * u, 2, m * (2 * GT) + n * GT, GT)

        @block.gpsimd
        def _(pool):
            pool.sem_inc(units_split, RING)
            pool.sem_inc(units_used, RING)
            pool.sem_inc(groups_evacuated, BANK_PAIRS)
            for s in (pv_made, st_made, cross_copied, o_normed, ab_made):
                pool.sem_inc(s, FREE)
            pool.memset(ident[:, :], 0.0).then_inc(setup_step, 1)
            pool.memset(all_mean[:, :], 1.0 / HG_DIM)
            pool.memset(eps[:, :], EPS)
            for h in range(HEADS):
                pool.memset(slopes[:, h:h + 1], 2.0 ** (-8.0 * (h + 1) / HEADS))
            pool.memset(tile_start[:, :], 1.0).then_inc(setup_step, 1)
            ints = SM[:, :, :].bitcast(I32)
            pool.iota(ints[:, 0, :], [[0, P]], base=0, channel_multiplier=1)
            pool.iota(ints[:, 1, :], [[1, P]], base=0, channel_multiplier=0)
            pool.iota(ints[:, 2, :], [[1, P]], base=0, channel_multiplier=-1)
            pool.iota(ints[:, 5, :], [[-1, P]], base=0, channel_multiplier=1)
            pool.iota(ints[:, 6:8, :].rearrange("p a b -> p (a b)"), [[-1, 2 * P]], base=P,
                      channel_multiplier=1)
            pool.wait_ge(setup_step, 2)
            pool.affine_select(out=ident[:, :], in_=ident[:, :], compare_op=ALU.not_equal, fill=1.0,
                               base=0, pattern=[[-1, P]], channel_multiplier=1)
            pool.memset(tile_start[:, :].rearrange("p (n w) -> p n w", w=P)[:, :, 0:1], 0.0)\
                .then_inc(pool_done, 1)
            pool.wait_ge(x_transposed, 2 * KT // 4)
            pool.memset(XK[:, :, :], 0.0).then_inc(xk_cleared, 1)

        @block.scalar
        def _(act):
            act.preload_act_table_set("natural_log_exp_and_others")
            act.dma_start(rows[0:2 * HG_HEADS, 0, :], lb_logits.rearrange("l (h c) -> (l h) c", c=P))\
                .then_inc(rows_loaded, 16)
            for i in range(2):
                s = slice(i * HEAD_DIM, (i + 1) * HEAD_DIM)
                act.dma_start(rows[2 * HG_HEADS:2 * HG_HEADS + 1, 0, s], q_norm).then_inc(rows_loaded, 16)
                act.dma_start(rows[K_GAIN:K_GAIN + 1, 0, s], k_norm).then_inc(rows_loaded, 16)
            act.dma_start(rows[HG_GAIN:HG_GAIN + 1, 0, :], hg_norm).then_inc(rows_loaded, 16)
            act.dma_start(rows[0:N_CONV, 1, :], conv_b.rearrange("a (r c) -> (a r) c", c=P))\
                .then_inc(rows_loaded, 16)
            for tap in range(CONV):
                act.dma_start(rows[0:N_CONV, 2 + tap, :],
                              conv_w[tap:tap + 1, :].rearrange("a (r c) -> (a r) c", c=P))\
                    .then_inc(rows_loaded, 16)
            act.dma_start(sink[:, :], sinks.broadcast_to([P, HEADS])).then_inc(rows_loaded, 16)
            act.wait_ge(pool_done, 1)

            def make_hi(quad, i):
                act.wait_ge(loaded[i], quad * 16 + 16)
                act.wait_ge(units_used, quad * RING + i + 1)
                act.copy(w_hi[:, i, :], raw[:, i, :]).then_inc(units_hi, 1)

            def norm_x(which):
                n = TT * which
                for t in range(TT):
                    if which == 0:
                        act.wait_ge(x_loaded[t], 16)
                    act.activation(hn[:, t, :], xt[:, t, :], ACT.Square, accum_out=ss[:, t:t + 1])\
                        .then_inc(x_squared, 1)
                    act.wait_ge(x_squared, n + t + 1)
                    act.activation(ss[:, t:t + 1], ss[:, t:t + 1], ACT.Ln, scale=1.0 / D_MODEL,
                                   bias=eps[:, :]).then_inc(x_rms, 1)
                    act.wait_ge(x_rms, n + t + 1)
                    act.activation(ss[:, t:t + 1], ss[:, t:t + 1], ACT.Exp, scale=-0.5).then_inc(x_rs, 1)
                    if which == 0 and t == 0:
                        for i in range(RING):
                            make_hi(0, i)
                for r in range(TT * KT // 4):
                    t, k = divmod(r, KT // 4)
                    act.wait_ge(x_transposed, which * TT * KT // 4 + r + 1)
                    act.copy(hs[:, 4 * k:4 * k + 4, t * P:(t + 1) * P],
                             bank[4 + r % 4][:, :].rearrange("p (k t) -> p k t", k=4)).then_inc(h_hi, 1)

            norm_x(0)
            act.wait_ge(param_step, 2)
            act.activation(lb_t[:, 1:3, :], lb_t[:, 1:3, :], ACT.Exp).then_inc(param_exp, 1)

            for i in range(RING):
                make_hi(1, i)

            def att_rms(a, width):
                act.wait_ge(att_mean, a + 1)
                act.activation(RS[:, 0:width], bank[7][:, 0:width], ACT.Ln, bias=eps[:, :])\
                    .then_inc(att_ln, 1)
                act.wait_ge(att_ln, a + 1)
                act.activation(RS[:, 0:width], RS[:, 0:width], ACT.Exp, scale=-0.5).then_inc(att_rs, 1)

            act.wait_ge(groups_evacuated, BANK_PAIRS + 1)
            act.activation(SQ[:, 0:SEQ], FE[:, 0, :], ACT.Square).then_inc(att_squared, 1)
            make_hi(2, 0)
            att_rms(0, SEQ)
            act.wait_ge(v_transposed, 1)
            act.copy(vt[:, :, :].rearrange("p t c -> p (t c)"), bank[6][:, 0:SEQ]).then_inc(vt_made, 1)
            for i in range(1, RING):
                make_hi(2, i)

            def exponentials(g, h):
                n = g * 4 + h
                act.wait_ge(top_made, n + 1)
                pr = PR[:, h % 2, :]
                act.activation(pr[:, 0:P], pr[:, 0:P], ACT.Exp, bias=top[:, h, 0:1],
                               accum_out=den[:, 0, h:h + 1])
                act.activation(pr[:, P:3 * P], pr[:, P:3 * P], ACT.Exp, bias=top[:, h, 1:2],
                               accum_out=den[:, 1, h:h + 1]).then_inc(exp_made, 1)
                act.activation(exp_sink[:, :, h], top[:, h, :], ACT.Exp, bias=sink[:, bass.ds(n, 1)])\
                    .then_inc(sink_made, 1)

            def copy_pt(g, h):
                n = g * 4 + h
                act.wait_ge(p_transposed, n + 1)
                act.wait_ge(pv_made, n + FREE)
                act.copy(PT[:, :], bank[6][:, 0:3 * P]).then_inc(pt_made, 1)

            def attention(g, quad):
                act.wait_ge(groups_evacuated, g + BANK_PAIRS + 2)
                act.activation(SQ[:, :], FE[:, :, :].rearrange("p a t -> p (a t)"), ACT.Square)\
                    .then_inc(att_squared, 1)
                att_rms(g + 1, 2 * SEQ)
                make_hi(quad, 0)
                make_hi(quad, 1)
                exponentials(g, 0)
                exponentials(g, 1)
                make_hi(quad, 2)
                copy_pt(g, 0)
                exponentials(g, 2)
                copy_pt(g, 1)
                exponentials(g, 3)
                make_hi(quad, 3)
                copy_pt(g, 2)
                copy_pt(g, 3)
                act.wait_ge(att_transposed, g + 1)
                act.copy(mix[:, bass.ds(g * 2, 2), 0:SEQ],
                         bank[6][:, :].rearrange("p (a t) -> p a t", a=2)).then_inc(att_hi, 1)

            with act.Fori(0, Q_GROUPS // 2) as i:
                for c in range(2):
                    attention(i * 2 + c, i * 2 + c + 3)

            def sigmoid(n):
                act.wait_ge(sg_clamped, n + 1)
                act.activation(SG[:, :], SG[:, :], ACT.Exp, scale=-1.0).then_inc(sg_exp, 1)
                act.wait_ge(sg_exp, n + 1)
                act.activation(SG[:, :], SG[:, :], ACT.Ln, bias=1.0).then_inc(sg_ln, 1)
                act.wait_ge(sg_ln, n + 1)
                act.activation(SG[:, :], SG[:, :], ACT.Exp, scale=-1.0).then_inc(sg_made, 1)

            def f_slot_of_next(j, quad):
                sigmoid(j * 3 + 2)
                make_hi(quad, 0)
                act.wait_ge(o_made, j + 1)
                act.activation(SQ[:, :], bank[6][:, :], ACT.Square).then_inc(o_squared, 1)
                make_hi(quad, 1)
                act.wait_ge(o_mean, j + 1)
                act.activation(RS[:, :], bank[7][:, :], ACT.Ln, bias=eps[:, :]).then_inc(o_ln, 1)
                act.wait_ge(o_ln, j + 1)
                act.activation(RS[:, :], RS[:, :], ACT.Exp, scale=-0.5).then_inc(o_rs, 1)
                make_hi(quad, 2)
                act.wait_ge(o_gated, j + 1)
                act.copy(mix[:, bass.ds(j * 2 + KT // 2, 2), 0:SEQ],
                         RS[:, :].rearrange("p (a t) -> p a t", a=2)).then_inc(hg_hi, 1)
                make_hi(quad, 3)

            def q_slot(j, quad):
                sigmoid(j * 3)
                make_hi(quad, 0)
                act.wait_ge(forget_made, j + 1)
                act.activation(LF[:, :], FE[:, :, :].rearrange("p a t -> p (a t)"), ACT.Ln)\
                    .then_inc(log_made, 1)
                for i in range(1, RING):
                    make_hi(quad, i)

            def i_slot(j, quad):
                act.wait_ge(exponents_made, j + 1)
                for half in range(2):
                    e = XQ[:, 4 * half:4 * half + 4, :]
                    act.activation(e, e, ACT.Exp).then_inc(decays_made, 1)
                sigmoid(j * 3 + 1)
                for i in range(RING):
                    make_hi(quad, i)

            def g_slot(j, quad):
                make_hi(quad, 0)
                act.wait_ge(i_transposed, j + 1)
                act.copy(V[:, :, :, :].rearrange("p h t c -> p (h t c)"), bank[6][:, :]).then_inc(v_made, 1)
                for i in range(1, RING):
                    make_hi(quad, i)
                act.wait_ge(cross_made, j + 1)
                act.copy(ST[:, :, 2, :], bank[4][:, 0:2 * P].rearrange("p (h t) -> p h t", h=2))\
                    .then_inc(cross_copied, 1)

            q_slot(0, G_F0 + 2)
            with act.Fori(0, PAIRS - 1) as j:
                i_slot(j, j * 4 + G_F0 + 3)
                g_slot(j, j * 4 + G_F0 + 4)
                f_slot_of_next(j, j * 4 + G_F0 + 5)
                q_slot(j + 1, j * 4 + G_F0 + 6)
            i_slot(PAIRS - 1, G_OUT - 1)
            g_slot(PAIRS - 1, Q_OUT)
            f_slot_of_next(PAIRS - 1, Q_OUT + 1)
            with act.Fori(Q_OUT + 2, Q_UP + 1) as quad:
                for i in range(RING):
                    make_hi(quad, i)
            act.wait_ge(groups_evacuated, BANK_PAIRS + G_UP)
            norm_x(1)
            act.preload_act_table_set("silu_and_others")
            for i in range(RING):
                make_hi(Q_UP + 1, i)

            def last_tap(n, ab, g):
                act.wait_ge(groups_evacuated, n + BANK_PAIRS + G_UP + 1)
                for c in range(2):
                    col = g * 2 + ab * (N_CONV // 2) + c
                    act.activation(C[:, ab, c, :], U[:, c, 2:SEQ + 2], ACT.Identity,
                                   scale=cols[:, bass.ds(col + conv_col(2), 1)],
                                   bias=cols[:, bass.ds(col + C_BIAS, 1)]).then_inc(tap2, 1)

            def a_work(g, quad):
                act.wait_ge(ab_made, g + FREE)
                last_tap(g * 2, 0, g)
                if quad is not None:
                    make_hi(quad, 0)
                act.wait_ge(tap0, g * 4 + 2)
                a = C[:, 0, :, :].rearrange("p c t -> p (c t)")
                act.activation(a, a, ACT.Silu).then_inc(silu_a, 1)
                for i in range(1, RING):
                    make_hi(quad, i)

            def b_work(g, quad):
                last_tap(g * 2 + 1, 1, g)
                for i in range(2):
                    make_hi(quad, i)
                act.wait_ge(ab_made, g + 1 + FREE)
                act.copy(gated[:, bass.ds(g * 2, 2), 0:SEQ], C[:, 1, :, :]).then_inc(gated_hi, 1)
                for i in range(2, RING):
                    make_hi(quad, i)

            with act.Fori(0, UP_GROUPS - 1) as g:
                a_work(g, g * 2 + Q_UP + 2)
                b_work(g, g * 2 + Q_UP + 3)
            a_work(UP_GROUPS - 1, Q_DOWN)
            b_work(UP_GROUPS - 1, Q_DOWN + 1)

            def store(n):
                act.wait_ge(groups_evacuated, n + BANK_PAIRS + G_DOWN + 1)
                act.dma_start(out_v[:, :, bass.ds(n * GT, GT)], xt[:, :, bass.ds(n * GT, GT)])\
                    .then_inc(stored, 16)

            for n in range(OUT_GROUPS):
                for u in range(n * DOWN_UNITS, (n + 1) * DOWN_UNITS):
                    if u >= 2 * RING:
                        make_hi(Q_DOWN + u // RING, u % RING)
                    if n and u == n * DOWN_UNITS + 2 * RING:
                        store(n - 1)
            store(OUT_GROUPS - 1)
            act.wait_ge(stored, 16 * OUT_GROUPS)

        @block.vector
        def _(dve):
            def make_lo(quad, i):
                dve.wait_ge(units_hi, quad * RING + i + 1)
                dve.tensor_tensor(w_lo[:, i, :], raw[:, i, :], w_hi[:, i, :].bitcast(F32), ALU.subtract)\
                    .then_inc(units_split, 1)

            def evacuate(group, units, dst):
                dve.wait_ge(units_used, units + RING)
                b0, b1 = pair_of(group)
                dve.tensor_reduce(dst[:, 0, :], b0[:, :].rearrange("p (h t) -> p t h", h=2), AX, ALU.add)
                dve.tensor_reduce(dst[:, 1, :], b1[:, :].rearrange("p (h t) -> p t h", h=2), AX, ALU.add)\
                    .then_inc(groups_evacuated, 1)

            def norm_x(which):
                n = which * TT
                dve.wait_ge(gain_loaded, 16 * (which + 1))
                for t in range(TT):
                    dve.wait_ge(x_rs, n + t + 1)
                    dve.scalar_tensor_tensor(hn[:, t, :], xt[:, t, :], ss[:, t:t + 1], gain[:, :],
                                             ALU.mult, ALU.mult).then_inc(x_normed, 1)
                    if which == 0 and t == 0:
                        for i in range(RING):
                            make_lo(0, i)
                for r in range(TT * KT // 4):
                    t, k = divmod(r, KT // 4)
                    dve.wait_ge(h_hi, which * TT * KT // 4 + r + 1)
                    dve.tensor_tensor(hs[:, 4 * k:4 * k + 4, SEQ + t * P:SEQ + (t + 1) * P],
                                      bank[4 + r % 4][:, :].rearrange("p (k t) -> p k t", k=4),
                                      hs[:, 4 * k:4 * k + 4, t * P:(t + 1) * P].bitcast(F32),
                                      ALU.subtract).then_inc(h_lo, 1)

            dve.memset(head_mean[:, :], 0.0).then_inc(mask_step, 1)
            dve.wait_ge(mask_step, 1)
            for h in range(2):
                s = slice(h * HEAD_DIM, (h + 1) * HEAD_DIM)
                dve.memset(head_mean[s, s], 1.0 / HEAD_DIM)
            dve.wait_ge(pool_done, 1)
            ints = SM[:, :, :].bitcast(I32)
            dve.tensor_tensor(ints[:, 3, :], ints[:, 0, :], ints[:, 1, :], ALU.bitwise_xor)\
                .then_inc(mask_step, 1)
            apart = ints[:, 5:8, :].rearrange("p a b -> p (a b)")
            dve.scalar_tensor_tensor(dist[:, :], apart, -1.0, apart, ALU.mult, ALU.min)\
                .then_inc(mask_step, 1)
            dve.tensor_scalar(SM[:, 4, :], ints[:, 2, :], 0.0, None, ALU.is_gt)
            dve.wait_ge(mask_step, 2)
            dve.tensor_copy(SM[:, 0, :], ints[:, 3, :]).then_inc(mask_step, 1)
            dve.wait_ge(mask_step, 4)
            for l in range(NL):
                dve.tensor_scalar(level_mask[:, l, :], SM[:, 0, :], float(LEVELS[l]), None, ALU.is_ge)
            dve.tensor_copy(level_mask[:, NL, :], ident[:, :]).then_inc(mask_step, 1)
            dve.wait_ge(mask_step, 5)
            for l in range(NL):
                dve.scalar_tensor_tensor(level_mask[:, l, :], SM[:, 0, :], 2.0 * LEVELS[l],
                                         level_mask[:, l, :], ALU.is_lt, ALU.mult)
            first, second = slice(0, CHUNK), slice(CHUNK, P)
            dve.memset(dist[first, CHUNK:P], FAR)
            dve.memset(dist[first, P:P + CHUNK], FAR)
            dve.memset(dist[first, P + 3 * CHUNK:P + 4 * CHUNK], FAR)
            dve.memset(dist[second, P:P + 2 * CHUNK], FAR).then_inc(mask_step, 1)
            dve.wait_ge(mask_step, 6)
            dve.tensor_tensor(level_mask[:, 0:NL, :], level_mask[:, 0:NL, :],
                              SM[:, 4:5, :].broadcast_to([P, NL, P]), ALU.mult).then_inc(masks_made, 1)

            norm_x(0)

            dve.wait_ge(rows_transposed, 1)
            dve.tensor_copy(cols[:, :], bank[0][:, 0:N_SMALL + (1 + CONV) * N_CONV]).then_inc(cols_made, 1)
            dve.wait_ge(cols_made, 1)
            l0, l1 = cols[:, 0:HG_HEADS], cols[:, HG_HEADS:2 * HG_HEADS]
            dve.tensor_scalar(q_gain[:, :], cols[:, 2 * HG_HEADS:2 * HG_HEADS + 1], HEAD_DIM ** -0.5,
                              None, ALU.mult)
            dve.tensor_tensor(lb_t[:, 0, :], l0, l1, ALU.max).then_inc(param_step, 1)
            dve.wait_ge(param_step, 1)
            dve.tensor_tensor(lb_t[:, 1, :], l0, lb_t[:, 0, :], ALU.subtract)
            dve.tensor_tensor(lb_t[:, 2, :], l1, lb_t[:, 0, :], ALU.subtract).then_inc(param_step, 1)
            dve.wait_ge(param_exp, 1)
            dve.tensor_tensor(lb_t[:, 3, :], lb_t[:, 1, :], lb_t[:, 2, :], ALU.add).then_inc(param_step, 1)
            dve.wait_ge(param_step, 3)
            dve.reciprocal(lb_t[:, 0, :], lb_t[:, 3, :]).then_inc(param_step, 1)
            dve.wait_ge(param_step, 4)
            dve.tensor_tensor(lb[:, :], lb_t[:, 1, :], lb_t[:, 0, :], ALU.mult).then_inc(param_step, 1)
            dve.wait_ge(param_step, 5)
            dve.tensor_scalar(one_lb[:, :], lb[:, :], -1.0, 1.0, ALU.mult, ALU.add).then_inc(params_made, 1)
            dve.wait_ge(params_made, 1)

            for i in range(RING):
                make_lo(1, i)

            evacuate(0, RING, FE)
            for half in range(2):
                dve.memset(kz[(1 - half) * HEAD_DIM:(2 - half) * HEAD_DIM, half::2, :], 0.0)\
                    .then_inc(kz_made, 1)
            make_lo(2, 0)
            dve.wait_ge(att_rs, 1)
            dve.scalar_tensor_tensor(QN[:, 0, :], FE[:, 0, :], cols[:, K_GAIN:K_GAIN + 1], RS[:, 0:SEQ],
                                     ALU.mult, ALU.mult).then_inc(qk_normed, 1)
            dve.wait_ge(qk_normed, 1)
            for g in range(KV_HEADS):
                for half in range(2):
                    dve.tensor_copy(kz[half * HEAD_DIM:(half + 1) * HEAD_DIM, 2 * g + half, :],
                                    QN[g * HEAD_DIM:(g + 1) * HEAD_DIM, 0, :]).then_inc(kz_made, 1)
            for i in range(1, RING):
                make_lo(2, i)

            def bias_and_max(g, h):
                n = g * 4 + h
                dve.wait_ge(scores_made, n + 1)
                pr = PR[:, h % 2, :]
                dve.scalar_tensor_tensor(pr, dist[:, :], slopes[:, bass.ds(n, 1)],
                                         bank[4 + h % 2][:, 0:3 * P], ALU.mult, ALU.add).then_inc(biased, 1)
                dve.wait_ge(biased, n + 1)
                dve.tensor_reduce(top[:, h, 0:1], pr[:, 0:P], AX, ALU.max)
                dve.tensor_reduce(top[:, h, 1:2], pr[:, P:3 * P], AX, ALU.max).then_inc(max_made, 1)
                dve.wait_ge(max_made, n + 1)
                dve.tensor_scalar(top[:, h, :], top[:, h, :], sink[:, bass.ds(n, 1)], -1.0,
                                  ALU.max, ALU.mult).then_inc(top_made, 1)

            def attention(g, parity, quad):
                evacuate(parity, (g + 2) * RING, FE)
                make_lo(quad, 0)
                dve.wait_ge(att_rs, g + 2)
                dve.scalar_tensor_tensor(QN[:, :, :].rearrange("p a t -> p (a t)"),
                                         FE[:, :, :].rearrange("p a t -> p (a t)"), q_gain[:, :],
                                         RS[:, :], ALU.mult, ALU.mult).then_inc(qk_normed, 1)
                make_lo(quad, 1)
                bias_and_max(g, 0)
                bias_and_max(g, 1)
                make_lo(quad, 2)
                bias_and_max(g, 2)
                bias_and_max(g, 3)
                make_lo(quad, 3)
                dve.wait_ge(sink_made, g * 4 + 4)
                dve.tensor_tensor(den[:, :, :], den[:, :, :], exp_sink[:, :, :], ALU.add)\
                    .then_inc(den_summed, 1)
                dve.wait_ge(den_summed, g + 1)
                dve.reciprocal(den[:, :, :], den[:, :, :]).then_inc(den_inverted, 1)
                dve.wait_ge(den_inverted, g + 1)
                dve.wait_ge(pv_made, g * 4 + 4 + FREE)
                dve.tensor_tensor(AO[:, :, :].rearrange("p t (h d) -> p (t h) d", h=4),
                                  bank[7][:, :].rearrange("p (a d) -> p a d", d=HEAD_DIM),
                                  den[:, :, :].rearrange("p t (h a) -> p (t h) a", a=1)
                                  .broadcast_to([P, TT * 4, HEAD_DIM]), ALU.mult).then_inc(att_scaled, 1)
                dve.wait_ge(att_hi, g + 1)
                dve.tensor_tensor(mix[:, bass.ds(g * 2, 2), SEQ:2 * SEQ],
                                  bank[6][:, :].rearrange("p (a t) -> p a t", a=2),
                                  mix[:, bass.ds(g * 2, 2), 0:SEQ].bitcast(F32), ALU.subtract)\
                    .then_inc(att_lo, 1)

            with dve.Fori(0, Q_GROUPS // 2) as i:
                for c in range(2):
                    attention(i * 2 + c, 1 + c, i * 2 + c + 3)

            def clamp(n, src):
                dve.tensor_scalar(SG[:, :], src[:, :, :].rearrange("p a t -> p (a t)"), SIG_MIN, None,
                                  ALU.max).then_inc(sg_clamped, 1)

            def f_slot_of_next(j, units, quad):
                evacuate(G_F0 + 3, units, GE)
                dve.wait_ge(groups_evacuated, j * 4 + G_F0 + 4 + BANK_PAIRS)
                clamp(j * 3 + 2, GE)
                make_lo(quad, 0)
                dve.wait_ge(sg_made, j * 3 + 3)
                ge = GE[:, :, :].rearrange("p a t -> p (a t)")
                dve.tensor_tensor(ge, ge, SG[:, :], ALU.mult).then_inc(silu_g, 1)
                make_lo(quad, 1)
                dve.wait_ge(o_rs, j + 1)
                dve.tensor_tensor(SQ[:, :], RS[:, :], bank[6][:, :], ALU.mult).then_inc(o_normed, 1)
                dve.wait_ge(o_normed, j + 1 + FREE)
                dve.scalar_tensor_tensor(RS[:, :], SQ[:, :], cols[:, HG_GAIN:HG_GAIN + 1], ge,
                                         ALU.mult, ALU.mult).then_inc(o_gated, 1)
                make_lo(quad, 2)
                dve.wait_ge(hg_hi, j + 1)
                rows_of = bass.ds(j * 2 + KT // 2, 2)
                dve.tensor_tensor(mix[:, rows_of, SEQ:2 * SEQ],
                                  RS[:, :].rearrange("p (a t) -> p a t", a=2),
                                  mix[:, rows_of, 0:SEQ].bitcast(F32), ALU.subtract).then_inc(hg_lo, 1)
                make_lo(quad, 3)

            def q_slot(j, group, quad):
                evacuate(G_F0, group * RING, FE)
                dve.wait_ge(groups_evacuated, group + BANK_PAIRS)
                clamp(j * 3, FE)
                make_lo(quad, 0)
                dve.wait_ge(sg_made, j * 3 + 1)
                for h in range(2):
                    dve.tensor_scalar(FE[:, h, :], SG[:, h * SEQ:(h + 1) * SEQ],
                                      one_lb[:, bass.ds(j * 2 + h, 1)], lb[:, bass.ds(j * 2 + h, 1)],
                                      ALU.mult, ALU.add).then_inc(forget_scaled, 1)
                dve.wait_ge(forget_scaled, j * 2 + 2)
                fe = FE[:, :, :].rearrange("p a t -> p (a t)")
                dve.tensor_scalar(fe, fe, FORGET_MIN, None, ALU.max).then_inc(forget_made, 1)
                dve.wait_ge(forget_made, j + 1)
                dve.tensor_scalar(K[:, :, :].rearrange("p a t -> p (a t)"), fe, -1.0, 1.0,
                                  ALU.mult, ALU.add).then_inc(k_made, 1)
                make_lo(quad, 1)
                dve.wait_ge(log_made, j + 1)
                dve.tensor_tensor_scan(B[:, :], tile_start[:, :], LF[:, :], 0.0, ALU.mult, ALU.add)\
                    .then_inc(sum_made, 1)
                make_lo(quad, 2)
                dve.wait_ge(sum_made, j + 1)
                for l in range(NL):
                    w = LEVELS[l]
                    b_left, b_right = halves(B[:, :], w)
                    x_left, x_right = halves(XQ[:, l, :], w)
                    r = b_left[:, :, w - 1:w].broadcast_to([P, 2 * SEQ // (2 * w), w])
                    dve.tensor_tensor(x_left, r, b_left, ALU.subtract)
                    dve.tensor_tensor(x_right, b_right, r, ALU.subtract)
                b_left, b_right = halves(B[:, :], P)
                x_left, x_right = halves(XQ[:, NL, :], P)
                r = b_left[:, :, P - 1:P].broadcast_to([P, 2, P])
                dve.tensor_tensor(x_left, r, b_left, ALU.subtract)
                dve.tensor_copy(x_right, b_right).then_inc(exponents_made, 1)
                make_lo(quad, 3)

            def i_slot(j, group, quad):
                evacuate(G_F0 + 1, group * RING, QE)
                dve.wait_ge(groups_evacuated, group + BANK_PAIRS)
                clamp(j * 3 + 1, QE)
                make_lo(quad, 0)
                k = K[:, :, :].rearrange("p a t -> p (a t)")
                dve.wait_ge(decays_made, j * 2 + 2)
                dve.wait_ge(xk_cleared, 1)
                for l in range(NL):
                    k_left, _ = halves(k, LEVELS[l])
                    e_left, _ = halves(XQ[:, l, :], LEVELS[l])
                    x_left, _ = halves(XK[:, l, :], LEVELS[l])
                    dve.tensor_tensor(x_left, k_left, e_left, ALU.mult)
                k_left, _ = halves(k, P)
                x_left, _ = halves(XQ[:, NL, :], P)
                dve.tensor_tensor(x_left, k_left, x_left, ALU.mult).then_inc(k_scaled, 1)
                make_lo(quad, 1)
                dve.wait_ge(sg_made, j * 3 + 2)
                q = QE[:, :, :].rearrange("p a t -> p (a t)")
                dve.tensor_tensor(q, q, SG[:, :], ALU.mult).then_inc(silu_q, 1)
                dve.wait_ge(silu_q, j + 1)
                for l in range(NL + 1):
                    w = (LEVELS + [P])[l]
                    _, q_right = halves(q, w)
                    _, x_right = halves(XQ[:, l, :], w)
                    last = dve.tensor_tensor(x_right, q_right, x_right, ALU.mult)
                last.then_inc(q_scaled, 1)
                make_lo(quad, 2)
                make_lo(quad, 3)

            def g_slot(j, group, quad):
                evacuate(G_F0 + 2, group * RING, IE)
                for r in range(2 * TT):
                    h, t = divmod(r, TT)
                    make_lo(quad, r)
                    dve.wait_ge(levels_made, j * 4 + r + 1)
                    dve.wait_ge(st_made, j * 4 + r + FREE)
                    for b in range(2):
                        dve.tensor_tensor(SM[:, 4 * b:4 * b + 4, :].rearrange("p l t -> p (l t)"),
                                          level_mask[:, 4 * b:4 * b + 4, :].rearrange("p l t -> p (l t)"),
                                          bank[4 + 2 * (r % 2) + b][:, :], ALU.mult).then_inc(masked, 1)
                    dve.wait_ge(masked, j * 8 + 2 * r + 2)
                    dve.tensor_reduce(ST[:, h, t, :], SM[:, :, :].rearrange("p l t -> p t l"), AX, ALU.add)\
                        .then_inc(st_made, 1)

            q_slot(0, G_F0 + 1, G_F0 + 2)
            with dve.Fori(0, PAIRS - 1) as j:
                i_slot(j, j * 4 + G_F0 + 2, j * 4 + G_F0 + 3)
                g_slot(j, j * 4 + G_F0 + 3, j * 4 + G_F0 + 4)
                f_slot_of_next(j, (j * 4 + G_F0 + 4) * RING, j * 4 + G_F0 + 5)
                q_slot(j + 1, j * 4 + G_F0 + 5, j * 4 + G_F0 + 6)
            i_slot(PAIRS - 1, G_OUT - 2, G_OUT - 1)
            g_slot(PAIRS - 1, G_OUT - 1, Q_OUT)
            f_slot_of_next(PAIRS - 1, G_OUT * RING, Q_OUT + 1)

            def add_to_x(group, units, n):
                dve.wait_ge(units_used, units + RING)
                c = bass.ds(n * GT, GT)
                for t in range(TT):
                    last = dve.tensor_tensor(xt[:, t, c], xt[:, t, c], pair_of(group)[t][:, :], ALU.add)
                last.then_inc(groups_evacuated, 1)

            for n in range(OUT_GROUPS):
                for c in range(QUADS_OUT):
                    quad = Q_OUT + n * QUADS_OUT + c
                    if n and c == 0:
                        add_to_x(G_OUT + n - 1, quad * RING, n - 1)
                    if quad > Q_OUT:
                        for i in range(RING):
                            make_lo(quad + 1, i)
            add_to_x(G_UP - 1, Q_UP * RING, OUT_GROUPS - 1)
            dve.memset(U[:, :, 0:2], 0.0).then_inc(u_cleared, 1)
            norm_x(1)
            for i in range(RING):
                make_lo(Q_UP + 1, i)

            def taps(n, ab, g, quad):
                dst = U[:, :, 2:SEQ + 2]
                evacuate(G_UP + ab, (n + Q_UP + 1) * RING, dst)
                for tap, before, after in ((1, tap2, tap1), (0, tap1, tap0)):
                    for c in range(2):
                        col = g * 2 + ab * (N_CONV // 2) + c + conv_col(tap)
                        dve.wait_ge(before, n * 2 + c + 1)
                        dve.scalar_tensor_tensor(C[:, ab, c, :], U[:, c, tap:tap + SEQ],
                                                 cols[:, bass.ds(col, 1)], C[:, ab, c, :],
                                                 ALU.mult, ALU.add).then_inc(after, 1)
                for i in range(2):
                    make_lo(quad, i)

            def a_work(g, quad):
                taps(g * 2, 0, g, quad)
                for i in range(2, RING):
                    make_lo(quad, i)

            def b_work(g, quad):
                taps(g * 2 + 1, 1, g, quad)
                dve.wait_ge(silu_a, g + 1)
                dve.wait_ge(tap0, g * 4 + 4)
                a = C[:, 0, :, :].rearrange("p c t -> p (c t)")
                b = C[:, 1, :, :].rearrange("p c t -> p (c t)")
                dve.tensor_tensor(b, a, b, ALU.mult).then_inc(ab_made, 1)
                make_lo(quad, 2)
                dve.wait_ge(gated_hi, g + 1)
                dve.tensor_tensor(gated[:, bass.ds(g * 2, 2), SEQ:2 * SEQ], C[:, 1, :, :],
                                  gated[:, bass.ds(g * 2, 2), 0:SEQ].bitcast(F32), ALU.subtract)\
                    .then_inc(gated_lo, 1)
                make_lo(quad, 3)

            with dve.Fori(0, UP_GROUPS - 1) as g:
                a_work(g, g * 2 + Q_UP + 2)
                b_work(g, g * 2 + Q_UP + 3)
            a_work(UP_GROUPS - 1, Q_DOWN)
            b_work(UP_GROUPS - 1, Q_DOWN + 1)
            for n in range(OUT_GROUPS):
                for u in range(n * DOWN_UNITS, (n + 1) * DOWN_UNITS):
                    if u >= 2 * RING:
                        make_lo(Q_DOWN + u // RING, u % RING)
                    if n and u == n * DOWN_UNITS + RING - 1:
                        add_to_x(G_DOWN + n - 1, Q_DOWN * RING + n * DOWN_UNITS, n - 1)
            add_to_x(G_DOWN + OUT_GROUPS - 1, Q_DOWN * RING + OUT_GROUPS * DOWN_UNITS, OUT_GROUPS - 1)

        @block.tensor
        def _(pe):
            def transpose(dst, src, n=P):
                return pe.transpose(dst, src, ident[0:n, 0:n])

            def norm_transposes(which):
                for r in range(TT * KT // 4):
                    t, k = divmod(r, KT // 4)
                    pe.wait_ge(x_normed, which * TT + t + 1)
                    if r >= 4:
                        pe.wait_ge(h_lo, which * TT * KT // 4 + r - 3)
                    for i in range(4):
                        last = transpose(bank[4 + r % 4][:, i * P:(i + 1) * P],
                                         hn[:, t, (4 * k + i) * P:(4 * k + i + 1) * P])
                    last.then_inc(x_transposed, 1)

            def unit_channels(quad, i, group):
                pe.wait_ge(units_split, quad * RING + i + 1 + RING)
                banks = pair_of(group)
                for k in range(4):
                    for b in range(2):
                        c = slice(k * GC + b * P, k * GC + (b + 1) * P)
                        x_k = hs[:, 4 * i + k, :]
                        pe.matmul(banks[b][:, :], w_hi[:, i, c], x_k, start=(i == 0 and k == 0), stop=False)
                        last = pe.matmul(banks[b][:, 0:SEQ], w_lo[:, i, c], x_k[:, 0:SEQ], start=False,
                                         stop=(i == RING - 1 and k == 3))
                last.then_inc(units_used, 1)

            def unit_tokens(quad, i, group, src, k0, k_all):
                pe.wait_ge(units_split, quad * RING + i + 1 + RING)
                banks = pair_of(group)
                for k in range(2):
                    hi, lo = w_hi[:, i, k * GT:(k + 1) * GT], w_lo[:, i, k * GT:(k + 1) * GT]
                    for t in range(TT):
                        x_hi = src[:, k0 + k, t * P:(t + 1) * P]
                        x_lo = src[:, k0 + k, SEQ + t * P:SEQ + (t + 1) * P]
                        pe.matmul(banks[t][:, :], x_hi, hi, start=(k0 + k == 0), stop=False)
                        pe.matmul(banks[t][:, :], x_hi, lo, start=False, stop=False)
                        last = pe.matmul(banks[t][:, :], x_lo, hi, start=False, stop=(k0 + k == k_all - 1))
                last.then_inc(units_used, 1)

            pe.wait_ge(pool_done, 1)
            pe.wait_ge(rows_loaded, 16 * (1 + 4 + 1 + 1 + CONV + 1))
            transpose(bank[0][:, 0:N_SMALL], rows[0:N_SMALL, 0, :], N_SMALL)
            for i in range(1 + CONV):
                at = N_SMALL + i * N_CONV
                last = transpose(bank[0][:, at:at + N_CONV], rows[0:N_CONV, 1 + i, :], N_CONV)
            last.then_inc(rows_transposed, 1)
            norm_transposes(0)
            pe.wait_ge(h_lo, TT * KT // 4)
            pe.wait_ge(cols_made, 1)

            for i in range(RING):
                unit_channels(0, i, 0)
            unit_channels(1, 0, 1)
            pe.wait_ge(att_squared, 1)
            pe.matmul(bank[7][:, 0:SEQ], head_mean[:, :], SQ[:, 0:SEQ], start=True, stop=True)\
                .then_inc(att_mean, 1)
            for t in range(TT):
                last = transpose(bank[6][:, t * P:(t + 1) * P], FE[:, 1, t * P:(t + 1) * P])
            last.then_inc(v_transposed, 1)
            for i in range(1, RING):
                unit_channels(1, i, 1)

            def scores(g, kv, h):
                a, half = divmod(h, 2)
                k = kz[:, bass.ds(kv * 2 + half, 1), :]
                out_b = bank[4 + h % 2]
                pe.matmul(out_b[:, 0:P], QN[:, a, 0:P], k[:, :, 0:P], start=True, stop=True)
                pe.matmul(out_b[:, P:3 * P], QN[:, a, P:2 * P], k, start=True, stop=True)\
                    .then_inc(scores_made, 1)

            def turn_p(g, h):
                n = g * 4 + h
                pe.wait_ge(exp_made, n + 1)
                if h:
                    pe.wait_ge(pt_made, n)
                for i in range(3):
                    last = transpose(bank[6][:, i * P:(i + 1) * P], PR[:, h % 2, i * P:(i + 1) * P])
                last.then_inc(p_transposed, 1)

            def times_v(g, kv, h):
                n = g * 4 + h
                pe.wait_ge(pt_made, n + 1)
                v = [vt[:, t, bass.ds(kv * HEAD_DIM, HEAD_DIM)] for t in range(TT)]
                o = [bank[7][:, (t * 4 + h) * HEAD_DIM:(t * 4 + h + 1) * HEAD_DIM] for t in range(TT)]
                pe.matmul(o[0], PT[:, 0:P], v[0], start=True, stop=True)
                pe.matmul(o[1], PT[:, P:2 * P], v[0], start=True, stop=False)
                pe.matmul(o[1], PT[:, 2 * P:3 * P], v[1], start=False, stop=True).then_inc(pv_made, 1)

            def attention(g, kv, quad, parity):
                pe.wait_ge(groups_evacuated, g + 2 + 1)
                unit_channels(quad, 0, parity)
                pe.wait_ge(att_squared, g + 2)
                pe.matmul(bank[7][:, :], head_mean[:, :], SQ[:, :], start=True, stop=True)\
                    .then_inc(att_mean, 1)
                unit_channels(quad, 1, parity)
                pe.wait_ge(qk_normed, g + 2)
                pe.wait_ge(kz_made, 6)
                scores(g, kv, 0)
                scores(g, kv, 1)
                unit_channels(quad, 2, parity)
                pe.wait_ge(vt_made, 1)
                turn_p(g, 0)
                times_v(g, kv, 0)
                pe.wait_ge(biased, g * 4 + 1)
                scores(g, kv, 2)
                turn_p(g, 1)
                times_v(g, kv, 1)
                pe.wait_ge(biased, g * 4 + 2)
                scores(g, kv, 3)
                unit_channels(quad, 3, parity)
                turn_p(g, 2)
                times_v(g, kv, 2)
                turn_p(g, 3)
                times_v(g, kv, 3)
                pe.wait_ge(att_scaled, g + 1)
                for a in range(2):
                    for t in range(TT):
                        last = transpose(bank[6][:, (a * TT + t) * P:(a * TT + t + 1) * P],
                                         AO[:, t, a * P:(a + 1) * P])
                last.then_inc(att_transposed, 1)

            with pe.Fori(0, Q_GROUPS // 2) as i:
                for c in range(2):
                    attention(i * 2 + c, i, i * 2 + c + 2, c)

            def plain_slot(group):
                pe.wait_ge(groups_evacuated, group + 1)
                for i in range(RING):
                    unit_channels(group, i, G_F0 + 1)

            def i_slot(j, group):
                pe.wait_ge(groups_evacuated, group + 1)
                for i in range(RING):
                    unit_channels(group, i, G_F0 + 2)

            def levels(j, r):
                h, t = divmod(r, TT)
                c = slice(h * SEQ + t * P, h * SEQ + (t + 1) * P)
                for l in range(NL + 1):
                    k = XK[:, l, c] if l < NL else K[:, h, t * P:(t + 1) * P]
                    q = XQ[:, l, c] if l < NL else QE[:, h, t * P:(t + 1) * P]
                    last = pe.matmul(bank[4 + 2 * (r % 2) + l // 4][:, (l % 4) * P:(l % 4 + 1) * P], k, q,
                                     start=True, stop=True)
                last.then_inc(levels_made, 1)

            def g_slot(j, group):
                pe.wait_ge(groups_evacuated, group + 1)
                unit_channels(group, 0, G_F0 + 3)
                pe.wait_ge(groups_evacuated, group + BANK_PAIRS)
                pe.wait_ge(o_normed, j + FREE)
                for h in range(2):
                    for t in range(TT):
                        last = transpose(bank[6][:, (h * TT + t) * P:(h * TT + t + 1) * P],
                                         IE[:, h, t * P:(t + 1) * P])
                last.then_inc(i_transposed, 1)
                pe.wait_ge(q_scaled, j + 1)
                pe.wait_ge(cross_copied, j + FREE)
                levels(j, 0)
                unit_channels(group, 1, G_F0 + 3)
                pe.wait_ge(v_made, j + 1)
                levels(j, 1)
                for r in range(2, 2 * TT):
                    unit_channels(group, r, G_F0 + 3)
                    pe.wait_ge(masked, j * 8 + 2 * (r - 1))
                    levels(j, r)
                pe.wait_ge(masked, j * 8 + 6)
                for h in range(2):
                    last = pe.matmul(bank[4][:, h * P:(h + 1) * P], XQ[:, NL, h * SEQ:h * SEQ + P],
                                     XQ[:, NL, h * SEQ + P:(h + 1) * SEQ], start=True, stop=True)
                last.then_inc(cross_made, 1)

            def output(j):
                pe.wait_ge(st_made, j * 4 + 4 + FREE)
                pe.wait_ge(cross_copied, j + 1 + FREE)
                for h in range(2):
                    o = h * SEQ
                    pe.matmul(bank[6][:, o:o + P], V[:, h, 0, :], ST[:, h, 0, :], start=True, stop=True)
                    pe.matmul(bank[6][:, o + P:o + SEQ], V[:, h, 0, :], ST[:, h, 2, :], start=True, stop=False)
                    last = pe.matmul(bank[6][:, o + P:o + SEQ], V[:, h, 1, :], ST[:, h, 1, :],
                                     start=False, stop=True)
                last.then_inc(o_made, 1)

            def output_mean(j):
                pe.wait_ge(o_squared, j + 1)
                pe.matmul(bank[7][:, :], all_mean[:, :], SQ[:, :], start=True, stop=True).then_inc(o_mean, 1)

            def f_slot_of_next(j, group):
                pe.wait_ge(groups_evacuated, group + 1)
                unit_channels(group, 0, G_F0)
                output(j)
                unit_channels(group, 1, G_F0)
                output_mean(j)
                unit_channels(group, 2, G_F0)
                unit_channels(group, 3, G_F0)

            plain_slot(G_F0 + 1)
            with pe.Fori(0, PAIRS - 1) as j:
                i_slot(j, j * 4 + G_F0 + 2)
                g_slot(j, j * 4 + G_F0 + 3)
                f_slot_of_next(j, j * 4 + G_F0 + 4)
                plain_slot(j * 4 + G_F0 + 5)
            i_slot(PAIRS - 1, G_OUT - 2)
            g_slot(PAIRS - 1, G_OUT - 1)

            pe.wait_ge(att_lo, Q_GROUPS)
            for n in range(OUT_GROUPS):
                pe.wait_ge(groups_evacuated, G_OUT + n + 1)
                for u in range(KT // 2):
                    if n == 0 and 2 * u >= KT // 2:
                        pe.wait_ge(hg_lo, u - KT // 4 + 1)
                    unit_tokens(Q_OUT + n * QUADS_OUT + u // RING, u % RING, G_OUT + n, mix, 2 * u, KT)
                    if n == 0 and u == 0:
                        output(PAIRS - 1)
                    if n == 0 and u == 1:
                        output_mean(PAIRS - 1)

            norm_transposes(1)
            pe.wait_ge(h_lo, 2 * TT * KT // 4)

            with pe.Fori(0, UP_GROUPS) as g:
                for ab in range(2):
                    pe.wait_ge(groups_evacuated, g * 2 + ab + G_UP + 1)
                    for i in range(RING):
                        unit_channels(g * 2 + ab + Q_UP, i, G_UP + ab)

            with pe.Fori(0, OUT_GROUPS // 2) as m:
                for v in range(2 * DOWN_UNITS):
                    n, u = divmod(v, DOWN_UNITS)
                    if u == 0:
                        pe.wait_ge(groups_evacuated, m * 2 + n + G_DOWN + 1)
                    if v == DOWN_UNITS - 1:
                        pe.wait_ge(gated_lo, UP_GROUPS)
                    unit_tokens(m * (2 * DOWN_UNITS // RING) + Q_DOWN + v // RING, v % RING,
                                G_DOWN + n, gated, 2 * u, KT_FF)


_INS = ["x", "attn_norm", "w_in", "q_norm", "k_norm", "attn_sinks", "hg_lb_logits", "hg_norm", "w_out",
        "ffn_norm", "w_ffn_up", "ffn_conv_w", "ffn_conv_b", "w_ffn_down"]
_LAYER = {"w_in", "w_out", "w_ffn_up", "ffn_conv_w", "w_ffn_down"}


def kernel(**inputs):
    import numpy as _np
    import concourse.bacc as _bacc
    from concourse import mybir as _mybir
    from concourse.bass_utils import run_bass_kernel_spmd as _run

    nc = _bacc.Bacc("TRN2", target_bir_lowering=False, num_devices=1)
    arrays, args = {}, []
    for name in _INS:
        a = _np.ascontiguousarray(inputs[name])
        if name in _LAYER or name == "x":
            a = a[0]
        arrays[f"in_{name}_dram"] = a
        args.append(nc.dram_tensor(f"in_{name}_dram", a.shape, _mybir.dt.from_np(a.dtype),
                                   kind="ExternalInput").ap())
    out = nc.dram_tensor("out_dram", (SEQ, D_MODEL), _mybir.dt.float32, kind="ExternalOutput").ap()
    hybrid_layer(nc, *args, out)
    r = _run(nc, [arrays], core_ids=[0])
    return r.results[0]["out_dram"].reshape(1, SEQ, D_MODEL)
```

```python
import concourse.bass as bass
from concourse import mybir
from contextlib import ExitStack

F32 = mybir.dt.float32
F32R = mybir.dt.float32r
I32 = mybir.dt.int32
ACT = mybir.ActivationFunctionType
ALU = mybir.AluOpType
AX = mybir.AxisListType.X

P = 128
D_MODEL, SEQ, CHUNK = 2048, 256, 64
EPS = 1e-6
HEADS, KV_HEADS, HEAD_DIM = 16, 2, 64
HG_HEADS, HG_DIM = 8, 128
D_FF, CONV = 5632, 3
KT = D_MODEL // P
KT_FF = D_FF // P
TT = SEQ // P
RING = 4
FREE = 1
BANK_PAIRS = 2
GC = 256
GT = 512
Q_GROUPS = HEADS * HEAD_DIM // GC
PAIRS = HG_HEADS // 2
COL_Q, COL_KV = 0, HEADS * HEAD_DIM
COL_HQ = COL_KV + 2 * KV_HEADS * HEAD_DIM
COL_HF = COL_HQ + HG_HEADS * HG_DIM
COL_HI = COL_HF + HG_HEADS * HG_DIM
COL_HG = COL_HI + HG_HEADS * HG_DIM
LEVELS = [2, 4, 8, 16, 32, 64]
MASKED_LEVELS = LEVELS[:-1] + [1]
NL = len(LEVELS)
HALF = P // 2
UP_GROUPS = D_FF // GC
OUT_GROUPS = D_MODEL // GT
Q_F0 = 1 + Q_GROUPS
QUADS_OUT = KT // 8
Q_OUT = Q_F0 + 4 * PAIRS
Q_UP = Q_OUT + QUADS_OUT * OUT_GROUPS
Q_DOWN = Q_UP + 2 * UP_GROUPS
DOWN_UNITS = KT_FF // 2
G_OUT = 0
G_UP = G_OUT + OUT_GROUPS
G_DOWN = G_UP + 2 * UP_GROUPS
FAR = -1e34
EXP_MAX = 2.0 ** 62
FORGET_MIN = 2.0 ** -63


def hybrid_layer(nc, x, attn_norm, w_in, q_norm, k_norm, sinks, lb_logits, hg_norm, w_out,
                 ffn_norm, w_up, conv_w, conv_b, w_down, out):
    ctx = ExitStack()
    with ctx:
        def sb(name, shape, dt=F32):
            return ctx.enter_context(nc.sbuf_tensor(name, shape, dt))

        def sem(name):
            return ctx.enter_context(nc.semaphore(name))

        xt = sb("xt", [P, TT, D_MODEL])
        hs = sb("hs", [P, KT, 2 * SEQ], F32R)
        raw = sb("raw", [P, RING, 1024])
        w_hi = sb("w_hi", [P, RING, 1024], F32R)
        w_lo = sb("w_lo", [P, RING, 1024], F32R)
        ident = sb("ident", [P, P])
        head_mean = sb("head_mean", [P, P])
        all_mean = sb("all_mean", [P, P])
        slopes = sb("slopes", [P, HEADS])
        sink = sb("sink", [P, HEADS])
        eps = sb("eps", [P, 1])
        rows = sb("rows", [P, 1 + 1 + CONV, P])
        N_SMALL = 2 * HG_HEADS + 3
        N_CONV = 2 * D_FF // P
        cols = sb("cols", [P, N_SMALL + (1 + CONV) * N_CONV])
        lb = sb("lb", [P, HG_HEADS])
        one_lb = sb("one_lb", [P, HG_HEADS])
        lb_t = sb("lb_t", [P, 4, HG_HEADS])
        q_gain = sb("q_gain", [P, 1])
        ss = sb("ss", [P, TT])
        K_GAIN = 2 * HG_HEADS + 1
        HG_GAIN = 2 * HG_HEADS + 2
        C_BIAS = N_SMALL

        def conv_col(tap):
            return N_SMALL + (1 + tap) * N_CONV

        def region(name, size):
            sb(name, [P, size // 4])
            return [nc.sbuf_base - size, nc.sbuf_base]

        def sb_at(place, name, shape, dt=F32):
            size = 4
            for n in shape[1:]:
                size *= n
            start = place[0]
            place[0] += size
            place[0] += -place[0] % 32
            assert place[0] <= place[1], name
            return nc.alloc_sbuf_tensor_at(name, shape, dt, offset=start)

        small = region("small_region", 8448)
        place = list(small)
        level_mask = sb_at(place, "level_mask", [P, NL, TT, HALF])
        same_mask = sb_at(place, "same_mask", [P, TT, P])
        tile_start = sb_at(place, "tile_start", [P, 2 * SEQ])
        dist = sb_at(place, "dist", [P, 3 * P])
        place = list(small)
        U = sb_at(place, "U", [P, 2, SEQ + 2])
        C = sb_at(place, "C", [P, 2, 2, SEQ])

        large = region("large_region", KT_FF * 2 * SEQ * 4)
        place = list(large)
        mix = sb_at(place, "mix", [P, KT, 2 * SEQ], F32R)
        FE = sb_at(place, "FE", [P, 2, SEQ])
        setup_place = list(place)
        QE = sb_at(place, "QE", [P, 2, SEQ])
        GE = sb_at(place, "GE", [P, 2, SEQ])
        IE = sb_at(place, "IE", [P, 2, SEQ])
        V = sb_at(place, "V", [P, 2, TT, P])
        SG = sb_at(place, "SG", [P, 2 * SEQ])
        SQ = sb_at(place, "SQ", [P, 2 * SEQ])
        RS = sb_at(place, "RS", [P, 2 * SEQ])
        ST = sb_at(place, "ST", [P, 2, 3, P])
        shared = list(place)
        K = sb_at(place, "K", [P, 2, SEQ])
        LF = sb_at(place, "LF", [P, 2 * SEQ])
        B = sb_at(place, "B", [P, 2 * SEQ])
        XK = sb_at(place, "XK", [P, NL, 2 * SEQ])
        Q1 = sb_at(place, "Q1", [P, 2 * SEQ // 2])
        attention_place = list(place)
        E = sb_at(place, "E", [P, NL + 1, 2, 2 * SEQ // 2])
        place = list(setup_place)
        SM = sb_at(place, "SM", [P, 8, P])
        mask_work = sb_at(place, "mask_work", [P, NL, P])
        place = list(attention_place)
        kz = sb_at(place, "kz", [P, KV_HEADS * 2, SEQ])
        vt = sb_at(place, "vt", [P, TT, P])
        QN = sb_at(place, "QN", [P, 2, SEQ])
        PR = sb_at(place, "PR", [P, 2, 3 * P])
        PT = sb_at(place, "PT", [P, 3 * P])
        AO = sb_at(place, "AO", [P, TT, 4 * HEAD_DIM])
        top = sb_at(place, "top", [P, 4, TT])
        exp_sink = sb_at(place, "exp_sink", [P, TT, 4])
        den = sb_at(place, "den", [P, TT, 4])
        place = list(shared)
        gain = sb_at(place, "gain", [P, D_MODEL])
        hn = sb_at(place, "hn", [P, TT, D_MODEL])
        place = list(large)
        gated = sb_at(place, "gated", [P, KT_FF, 2 * SEQ], F32R)

        bank = [ctx.enter_context(nc.psum_tensor(f"bank{i}", [P, 512], F32)) for i in range(8)]

        loaded = [sem(f"loaded{i}") for i in range(RING)]
        units_hi = sem("units_hi")
        units_split = sem("units_split")
        units_used = sem("units_used")
        groups_evacuated = sem("groups_evacuated")
        x_loaded = [sem(f"x_loaded{t}") for t in range(TT)]
        gain_loaded, rows_loaded = sem("gain_loaded"), sem("rows_loaded")
        pool_done, masks_made, cols_made, params_made = (
            sem("pool_done"), sem("masks_made"), sem("cols_made"), sem("params_made"))
        setup_step, mask_step = sem("setup_step"), sem("mask_step")
        param_step, param_exp = sem("param_step"), sem("param_exp")
        rows_transposed, xk_cleared = sem("rows_transposed"), sem("xk_cleared")
        x_squared, x_rms, x_rs, x_normed = sem("x_squared"), sem("x_rms"), sem("x_rs"), sem("x_normed")
        x_transposed, h_hi, h_lo = sem("x_transposed"), sem("h_hi"), sem("h_lo")
        att_squared, att_mean, att_ln, att_rs, qk_normed = (
            sem("att_squared"), sem("att_mean"), sem("att_ln"), sem("att_rs"), sem("qk_normed"))
        kz_made, v_copied, v_transposed, vt_made = (
            sem("kz_made"), sem("v_copied"), sem("v_transposed"), sem("vt_made"))
        scores_made, biased, max_made, top_made = (
            sem("scores_made"), sem("biased"), sem("max_made"), sem("top_made"))
        exp_made, p_transposed, pt_made, pv_made = (
            sem("exp_made"), sem("p_transposed"), sem("pt_made"), sem("pv_made"))
        sink_made, den_summed, den_inverted, att_scaled = (
            sem("sink_made"), sem("den_summed"), sem("den_inverted"), sem("att_scaled"))
        att_transposed, att_hi, att_lo = sem("att_transposed"), sem("att_hi"), sem("att_lo")
        sg_clamped, sg_exp, sg_ln, sg_made = (
            sem("sg_clamped"), sem("sg_exp"), sem("sg_ln"), sem("sg_made"))
        forget_scaled, forget_made, log_made, k_made, sum_made = (
            sem("forget_scaled"), sem("forget_made"), sem("log_made"), sem("k_made"), sem("sum_made"))
        exponents_made, decays_made, k_scaled, silu_q, q_scaled, silu_g = (
            sem("exponents_made"), sem("decays_made"), sem("k_scaled"), sem("silu_q"),
            sem("q_scaled"), sem("silu_g"))
        i_copied, i_transposed, v_made, levels_made, st_written, st_turn, st_made = (
            sem("i_copied"), sem("i_transposed"), sem("v_made"), sem("levels_made"),
            sem("st_written"), sem("st_turn"), sem("st_made"))
        o_made, o_squared, o_mean, o_ln, o_rs = (
            sem("o_made"), sem("o_squared"), sem("o_mean"), sem("o_ln"), sem("o_rs"))
        o_normed, o_gated, hg_hi, hg_lo = sem("o_normed"), sem("o_gated"), sem("hg_hi"), sem("hg_lo")
        u_cleared, tap2, tap1, tap0 = sem("u_cleared"), sem("tap2"), sem("tap1"), sem("tap0")
        silu_a, ab_made, gated_hi, gated_lo = (
            sem("silu_a"), sem("ab_made"), sem("gated_hi"), sem("gated_lo"))
        stored = sem("stored")

        w_in_v = w_in.rearrange("(k p) n -> p k n", p=P)
        w_out_v = w_out.rearrange("(k p) n -> p k n", p=P)
        w_up_v = w_up.rearrange("(k p) n -> p k n", p=P)
        w_down_v = w_down.rearrange("(k p) n -> p k n", p=P)
        x_v = x.rearrange("(t p) n -> p t n", p=P)
        out_v = out.rearrange("(t p) n -> p t n", p=P)

        def pair_of(group):
            b = 2 * ((group + 1) % BANK_PAIRS)
            return bank[b], bank[b + 1]

        bank_f = bank_i = bank[1]
        bank_q = bank_g = bank[0]
        bank_scores = [bank[2:5], bank[5:8]]
        bank_o, bank_mean, bank_v = bank[6], bank[7], bank[7]
        SAME, CROSS = slice(0, 2 * P), slice(2 * P, 3 * P)

        def level_columns(l):
            return l // 4, (l % 4) * P

        def halves(ap, width):
            v = ap.rearrange("p (n two w) -> p n two w", two=2, w=width)
            return v[:, :, 0, :], v[:, :, 1, :]

        block = ctx.enter_context(nc.Block())

        @block.sync
        def _(sp):
            for t in range(TT):
                sp.dma_start(xt[:, t, :], x_v[:, t, :]).then_inc(x_loaded[t], 16)
                if t == 0:
                    sp.dma_start(gain[:, :], attn_norm.broadcast_to([P, D_MODEL])).then_inc(gain_loaded, 16)

            def load_unit(quad, i, view, row, rows_n, col, cols_n):
                sp.wait_ge(units_split, quad * RING + i + 1)
                sp.dma_start(raw[:, i, :].rearrange("p (k n) -> p k n", k=rows_n),
                             view[:, row:row + rows_n, bass.ds(col, cols_n)]).then_inc(loaded[i], 16)

            def load_channels(quad, view, col):
                for i in range(RING):
                    load_unit(quad, i, view, 4 * i, 4, col, GC)

            load_channels(0, w_in_v, COL_KV)
            with sp.Fori(0, Q_GROUPS) as g:
                load_channels(g + 1, w_in_v, g * GC + COL_Q)
            load_channels(Q_F0, w_in_v, COL_HF)
            load_channels(Q_F0 + 1, w_in_v, COL_HQ)
            with sp.Fori(0, PAIRS - 1) as j:
                load_channels(j * 4 + Q_F0 + 2, w_in_v, j * GC + COL_HI)
                load_channels(j * 4 + Q_F0 + 3, w_in_v, j * GC + COL_HG)
                load_channels(j * 4 + Q_F0 + 4, w_in_v, j * GC + COL_HF + GC)
                load_channels(j * 4 + Q_F0 + 5, w_in_v, j * GC + COL_HQ + GC)
            load_channels(Q_OUT - 2, w_in_v, COL_HI + (PAIRS - 1) * GC)
            load_channels(Q_OUT - 1, w_in_v, COL_HG + (PAIRS - 1) * GC)
            with sp.Fori(0, OUT_GROUPS) as n:
                for c in range(QUADS_OUT):
                    for i in range(RING):
                        load_unit(n * QUADS_OUT + Q_OUT + c, i, w_out_v, 8 * c + 2 * i, 2, n * GT, GT)
            sp.wait_ge(levels_made, 2 * PAIRS)
            sp.dma_start(gain[:, :], ffn_norm.broadcast_to([P, D_MODEL])).then_inc(gain_loaded, 16)
            with sp.Fori(0, UP_GROUPS) as g:
                load_channels(g * 2 + Q_UP, w_up_v, g * GC)
                load_channels(g * 2 + Q_UP + 1, w_up_v, g * GC + D_FF)
            with sp.Fori(0, OUT_GROUPS // 2) as m:
                for v in range(2 * DOWN_UNITS):
                    n, u = divmod(v, DOWN_UNITS)
                    load_unit(m * (2 * DOWN_UNITS // RING) + Q_DOWN + v // RING, v % RING,
                              w_down_v, 2 * u, 2, m * (2 * GT) + n * GT, GT)

        @block.gpsimd
        def _(pool):
            pool.sem_inc(units_split, RING)
            pool.sem_inc(units_used, RING)
            pool.sem_inc(groups_evacuated, BANK_PAIRS)
            for s in (pv_made, st_made, o_normed, ab_made):
                pool.sem_inc(s, FREE)
            pool.memset(ident[:, :], 0.0).then_inc(setup_step, 1)
            pool.memset(all_mean[:, :], 1.0 / HG_DIM)
            pool.memset(eps[:, :], EPS)
            for h in range(HEADS):
                pool.memset(slopes[:, h:h + 1], 2.0 ** (-8.0 * (h + 1) / HEADS))
            pool.memset(tile_start[:, :], 1.0).then_inc(setup_step, 1)
            ints = SM[:, :, :].bitcast(I32)
            pool.iota(ints[:, 0, :], [[0, P]], base=0, channel_multiplier=1)
            pool.iota(ints[:, 1, :], [[1, P]], base=0, channel_multiplier=0)
            pool.iota(ints[:, 2, :], [[1, P]], base=0, channel_multiplier=-1)
            pool.iota(ints[:, 5, :], [[-1, P]], base=0, channel_multiplier=1)
            pool.iota(ints[:, 6:8, :].rearrange("p a b -> p (a b)"), [[-1, 2 * P]], base=P,
                      channel_multiplier=1)
            pool.wait_ge(setup_step, 2)
            pool.affine_select(out=ident[:, :], in_=ident[:, :], compare_op=ALU.not_equal, fill=1.0,
                               base=0, pattern=[[-1, P]], channel_multiplier=1)
            pool.memset(tile_start[:, :].rearrange("p (n w) -> p n w", w=P)[:, :, 0:1], 0.0)\
                .then_inc(pool_done, 1)
            pool.memset(ST[:, :, :, :], 0.0)
            pool.wait_ge(x_transposed, 2 * KT // 4)
            pool.memset(XK[:, :, :], 0.0).then_inc(xk_cleared, 1)

        @block.scalar
        def _(act):
            act.preload_act_table_set("natural_log_exp_and_others")
            act.dma_start(rows[0:2 * HG_HEADS, 0, :], lb_logits.rearrange("l (h c) -> (l h) c", c=P))\
                .then_inc(rows_loaded, 16)
            for i in range(2):
                s = slice(i * HEAD_DIM, (i + 1) * HEAD_DIM)
                act.dma_start(rows[2 * HG_HEADS:2 * HG_HEADS + 1, 0, s], q_norm).then_inc(rows_loaded, 16)
                act.dma_start(rows[K_GAIN:K_GAIN + 1, 0, s], k_norm).then_inc(rows_loaded, 16)
            act.dma_start(rows[HG_GAIN:HG_GAIN + 1, 0, :], hg_norm).then_inc(rows_loaded, 16)
            act.dma_start(rows[0:N_CONV, 1, :], conv_b.rearrange("a (r c) -> (a r) c", c=P))\
                .then_inc(rows_loaded, 16)
            for tap in range(CONV):
                act.dma_start(rows[0:N_CONV, 2 + tap, :],
                              conv_w[tap:tap + 1, :].rearrange("a (r c) -> (a r) c", c=P))\
                    .then_inc(rows_loaded, 16)
            act.dma_start(sink[:, :], sinks.broadcast_to([P, HEADS])).then_inc(rows_loaded, 16)
            act.wait_ge(pool_done, 1)

            def make_hi(quad, i):
                act.wait_ge(loaded[i], quad * 16 + 16)
                act.wait_ge(units_used, quad * RING + i + 1)
                act.copy(w_hi[:, i, :], raw[:, i, :]).then_inc(units_hi, 1)

            def norm_x(which):
                n = TT * which
                for t in range(TT):
                    if which == 0:
                        act.wait_ge(x_loaded[t], 16)
                    act.activation(hn[:, t, :], xt[:, t, :], ACT.Square, accum_out=ss[:, t:t + 1])\
                        .then_inc(x_squared, 1)
                    act.wait_ge(x_squared, n + t + 1)
                    act.activation(ss[:, t:t + 1], ss[:, t:t + 1], ACT.Ln, scale=1.0 / D_MODEL,
                                   bias=eps[:, :]).then_inc(x_rms, 1)
                    act.wait_ge(x_rms, n + t + 1)
                    act.activation(ss[:, t:t + 1], ss[:, t:t + 1], ACT.Exp, scale=-0.5).then_inc(x_rs, 1)
                    if which == 0 and t == 0:
                        for i in range(RING):
                            make_hi(0, i)
                for r in range(TT * KT // 4):
                    t, k = divmod(r, KT // 4)
                    act.wait_ge(x_transposed, which * TT * KT // 4 + r + 1)
                    act.copy(hs[:, 4 * k:4 * k + 4, t * P:(t + 1) * P],
                             bank[4 + r % 4][:, :].rearrange("p (k t) -> p k t", k=4)).then_inc(h_hi, 1)

            norm_x(0)
            act.wait_ge(param_step, 2)
            act.activation(lb_t[:, 1:3, :], lb_t[:, 1:3, :], ACT.Exp).then_inc(param_exp, 1)

            for i in range(RING):
                make_hi(1, i)

            def att_rms(a, width):
                act.wait_ge(att_mean, a + 1)
                act.activation(RS[:, 0:width], bank[7][:, 0:width], ACT.Ln, bias=eps[:, :])\
                    .then_inc(att_ln, 1)
                act.wait_ge(att_ln, a + 1)
                act.activation(RS[:, 0:width], RS[:, 0:width], ACT.Exp, scale=-0.5).then_inc(att_rs, 1)

            act.wait_ge(units_used, 2 * RING)
            act.activation(SQ[:, 0:SEQ], bank[0][:, 0:SEQ], ACT.Square).then_inc(att_squared, 1)
            act.copy(FE[:, 1, :], bank[0][:, SEQ:2 * SEQ]).then_inc(v_copied, 1)
            make_hi(2, 0)
            att_rms(0, SEQ)
            act.wait_ge(v_transposed, 1)
            act.copy(vt[:, :, :].rearrange("p t c -> p (t c)"), bank[6][:, 0:SEQ]).then_inc(vt_made, 1)
            for i in range(1, RING):
                make_hi(2, i)

            def exponentials(g, h):
                n = g * 4 + h
                act.wait_ge(top_made, n + 1)
                pr = PR[:, h % 2, :]
                act.activation(pr[:, 0:P], pr[:, 0:P], ACT.Exp, bias=top[:, h, 0:1],
                               accum_out=den[:, 0, h:h + 1])
                act.activation(pr[:, P:3 * P], pr[:, P:3 * P], ACT.Exp, bias=top[:, h, 1:2],
                               accum_out=den[:, 1, h:h + 1]).then_inc(exp_made, 1)
                act.activation(exp_sink[:, :, h], top[:, h, :], ACT.Exp, bias=sink[:, bass.ds(n, 1)])\
                    .then_inc(sink_made, 1)

            def copy_pt(g, h):
                n = g * 4 + h
                act.wait_ge(p_transposed, n + 1)
                act.wait_ge(pv_made, n + FREE)
                act.copy(PT[:, :], bank[6][:, 0:3 * P]).then_inc(pt_made, 1)

            def attention(g, q_bank, quad):
                act.wait_ge(units_used, (g + 3) * RING)
                act.activation(SQ[:, :], q_bank[:, :], ACT.Square).then_inc(att_squared, 1)
                att_rms(g + 1, 2 * SEQ)
                make_hi(quad, 0)
                make_hi(quad, 1)
                exponentials(g, 0)
                exponentials(g, 1)
                make_hi(quad, 2)
                copy_pt(g, 0)
                exponentials(g, 2)
                copy_pt(g, 1)
                exponentials(g, 3)
                make_hi(quad, 3)
                copy_pt(g, 2)
                copy_pt(g, 3)
                act.wait_ge(att_transposed, g + 1)
                act.copy(mix[:, bass.ds(g * 2, 2), 0:SEQ],
                         bank[6][:, :].rearrange("p (a t) -> p a t", a=2)).then_inc(att_hi, 1)

            with act.Fori(0, Q_GROUPS // 2) as i:
                for c in range(2):
                    attention(i * 2 + c, bank[1 - c], i * 2 + c + 3)

            def sigmoid_exp(n, src, quad):
                act.wait_ge(units_used, (quad + 2) * RING)
                act.activation(SG[:, :], src[:, :], ACT.Exp, scale=-1.0).then_inc(sg_exp, 1)

            def sigmoid_rest(n):
                act.wait_ge(sg_clamped, n + 1)
                act.activation(SG[:, :], SG[:, :], ACT.Ln, bias=1.0).then_inc(sg_ln, 1)
                act.wait_ge(sg_ln, n + 1)
                act.activation(SG[:, :], SG[:, :], ACT.Exp, scale=-1.0).then_inc(sg_made, 1)


            def q_slot(j, quad):
                sigmoid_exp(j * 3, bank_f, quad - 1)
                make_hi(quad + 1, 0)
                sigmoid_rest(j * 3)
                act.wait_ge(sg_made, j * 3 + 1)
                for h in range(2):
                    act.activation(FE[:, h, :], SG[:, h * SEQ:(h + 1) * SEQ], ACT.Identity,
                                   scale=one_lb[:, bass.ds(j * 2 + h, 1)],
                                   bias=lb[:, bass.ds(j * 2 + h, 1)]).then_inc(forget_scaled, 1)
                make_hi(quad + 1, 1)
                act.wait_ge(forget_made, j + 1)
                act.activation(LF[:, :], FE[:, :, :].rearrange("p a t -> p (a t)"), ACT.Ln)\
                    .then_inc(log_made, 1)
                make_hi(quad + 1, 2)
                make_hi(quad + 1, 3)
                act.wait_ge(exponents_made, j * 2 + 1)
                e = E[:, 0:4, :, :]
                act.activation(e, e, ACT.Exp).then_inc(decays_made, 1)

            def i_slot(j, quad):
                sigmoid_exp(j * 3 + 1, bank_q, quad - 1)
                make_hi(quad + 1, 0)
                act.wait_ge(exponents_made, j * 2 + 2)
                act.activation(E[:, NL, 1, :].rearrange("p (h t) -> p h t", h=2),
                               halves(B[:, :], P)[1], ACT.Exp)
                act.activation(E[:, 4:NL, :, :], E[:, 4:NL, :, :], ACT.Exp)
                act.activation(E[:, NL, 0, :], E[:, NL, 0, :], ACT.Exp).then_inc(decays_made, 1)
                sigmoid_rest(j * 3 + 1)
                for i in range(1, RING):
                    make_hi(quad + 1, i)

            def g_slot(j, quad):
                act.wait_ge(units_used, (quad + 1) * RING)
                act.copy(IE[:, :, :].rearrange("p a t -> p (a t)"), bank_i[:, :]).then_inc(i_copied, 1)
                make_hi(quad + 1, 0)
                make_hi(quad + 1, 1)
                act.wait_ge(i_transposed, j + 1)
                act.copy(V[:, :, :, :].rearrange("p h t c -> p (h t c)"), bank_v[:, :]).then_inc(v_made, 1)
                make_hi(quad + 1, 2)
                make_hi(quad + 1, 3)

            def f_slot_of_next(j, quad):
                sigmoid_exp(j * 3 + 2, bank_g, quad - 1)
                make_hi(quad + 1, 0)
                sigmoid_rest(j * 3 + 2)
                act.wait_ge(o_made, j + 1)
                act.activation(SQ[:, :], bank_o[:, :], ACT.Square).then_inc(o_squared, 1)
                make_hi(quad + 1, 1)
                act.wait_ge(o_mean, j + 1)
                act.activation(RS[:, :], bank_mean[:, :], ACT.Ln, bias=eps[:, :]).then_inc(o_ln, 1)
                act.wait_ge(o_ln, j + 1)
                act.activation(RS[:, :], RS[:, :], ACT.Exp, scale=-0.5).then_inc(o_rs, 1)
                make_hi(quad + 1, 2)
                make_hi(quad + 1, 3)
                act.wait_ge(o_gated, j + 1)
                act.copy(mix[:, bass.ds(j * 2 + KT // 2, 2), 0:SEQ],
                         RS[:, :].rearrange("p (a t) -> p a t", a=2)).then_inc(hg_hi, 1)

            q_slot(0, Q_F0 + 1)
            with act.Fori(0, PAIRS - 1) as j:
                i_slot(j, j * 4 + Q_F0 + 2)
                g_slot(j, j * 4 + Q_F0 + 3)
                f_slot_of_next(j, j * 4 + Q_F0 + 4)
                q_slot(j + 1, j * 4 + Q_F0 + 5)
            i_slot(PAIRS - 1, Q_OUT - 2)
            g_slot(PAIRS - 1, Q_OUT - 1)
            f_slot_of_next(PAIRS - 1, Q_OUT)
            with act.Fori(Q_OUT + 2, Q_UP + 1) as quad:
                for i in range(RING):
                    make_hi(quad, i)
            act.wait_ge(groups_evacuated, BANK_PAIRS + G_UP)
            norm_x(1)
            act.preload_act_table_set("silu_and_others")
            for i in range(RING):
                make_hi(Q_UP + 1, i)

            def last_tap(n, ab, g):
                act.wait_ge(groups_evacuated, n + BANK_PAIRS + G_UP + 1)
                for c in range(2):
                    col = g * 2 + ab * (N_CONV // 2) + c
                    act.activation(C[:, ab, c, :], U[:, c, 2:SEQ + 2], ACT.Identity,
                                   scale=cols[:, bass.ds(col + conv_col(2), 1)],
                                   bias=cols[:, bass.ds(col + C_BIAS, 1)]).then_inc(tap2, 1)

            def a_work(g, quad):
                act.wait_ge(ab_made, g + FREE)
                last_tap(g * 2, 0, g)
                if quad is not None:
                    make_hi(quad, 0)
                act.wait_ge(tap0, g * 4 + 2)
                a = C[:, 0, :, :].rearrange("p c t -> p (c t)")
                act.activation(a, a, ACT.Silu).then_inc(silu_a, 1)
                for i in range(1, RING):
                    make_hi(quad, i)

            def b_work(g, quad):
                last_tap(g * 2 + 1, 1, g)
                for i in range(2):
                    make_hi(quad, i)
                act.wait_ge(ab_made, g + 1 + FREE)
                act.copy(gated[:, bass.ds(g * 2, 2), 0:SEQ], C[:, 1, :, :]).then_inc(gated_hi, 1)
                for i in range(2, RING):
                    make_hi(quad, i)

            with act.Fori(0, UP_GROUPS - 1) as g:
                a_work(g, g * 2 + Q_UP + 2)
                b_work(g, g * 2 + Q_UP + 3)
            a_work(UP_GROUPS - 1, Q_DOWN)
            b_work(UP_GROUPS - 1, Q_DOWN + 1)

            def store(n):
                act.wait_ge(groups_evacuated, n + BANK_PAIRS + G_DOWN + 1)
                act.dma_start(out_v[:, :, bass.ds(n * GT, GT)], xt[:, :, bass.ds(n * GT, GT)])\
                    .then_inc(stored, 16)

            for n in range(OUT_GROUPS):
                for u in range(n * DOWN_UNITS, (n + 1) * DOWN_UNITS):
                    if u >= 2 * RING:
                        make_hi(Q_DOWN + u // RING, u % RING)
                    if n and u == n * DOWN_UNITS + 2 * RING:
                        store(n - 1)
            store(OUT_GROUPS - 1)
            act.wait_ge(stored, 16 * OUT_GROUPS)

        @block.vector
        def _(dve):
            def make_lo(quad, i):
                dve.wait_ge(units_hi, quad * RING + i + 1)
                dve.tensor_tensor(w_lo[:, i, :], raw[:, i, :], w_hi[:, i, :].bitcast(F32), ALU.subtract)\
                    .then_inc(units_split, 1)

            def evacuate(group, units, dst):
                dve.wait_ge(units_used, units + RING)
                b0, b1 = pair_of(group)
                dve.tensor_reduce(dst[:, 0, :], b0[:, :].rearrange("p (h t) -> p t h", h=2), AX, ALU.add)
                dve.tensor_reduce(dst[:, 1, :], b1[:, :].rearrange("p (h t) -> p t h", h=2), AX, ALU.add)\
                    .then_inc(groups_evacuated, 1)

            def norm_x(which):
                n = which * TT
                dve.wait_ge(gain_loaded, 16 * (which + 1))
                for t in range(TT):
                    dve.wait_ge(x_rs, n + t + 1)
                    dve.scalar_tensor_tensor(hn[:, t, :], xt[:, t, :], ss[:, t:t + 1], gain[:, :],
                                             ALU.mult, ALU.mult).then_inc(x_normed, 1)
                    if which == 0 and t == 0:
                        for i in range(RING):
                            make_lo(0, i)
                for r in range(TT * KT // 4):
                    t, k = divmod(r, KT // 4)
                    dve.wait_ge(h_hi, which * TT * KT // 4 + r + 1)
                    dve.tensor_tensor(hs[:, 4 * k:4 * k + 4, SEQ + t * P:SEQ + (t + 1) * P],
                                      bank[4 + r % 4][:, :].rearrange("p (k t) -> p k t", k=4),
                                      hs[:, 4 * k:4 * k + 4, t * P:(t + 1) * P].bitcast(F32),
                                      ALU.subtract).then_inc(h_lo, 1)

            dve.memset(head_mean[:, :], 0.0).then_inc(mask_step, 1)
            dve.wait_ge(mask_step, 1)
            for h in range(2):
                s = slice(h * HEAD_DIM, (h + 1) * HEAD_DIM)
                dve.memset(head_mean[s, s], 1.0 / HEAD_DIM)
            dve.wait_ge(pool_done, 1)
            ints = SM[:, :, :].bitcast(I32)
            dve.tensor_tensor(ints[:, 3, :], ints[:, 0, :], ints[:, 1, :], ALU.bitwise_xor)\
                .then_inc(mask_step, 1)
            apart = ints[:, 5:8, :].rearrange("p a b -> p (a b)")
            dve.scalar_tensor_tensor(dist[:, :], apart, -1.0, apart, ALU.mult, ALU.min)\
                .then_inc(mask_step, 1)
            dve.tensor_scalar(SM[:, 4, :], ints[:, 2, :], 0.0, None, ALU.is_gt)
            dve.wait_ge(mask_step, 2)
            dve.tensor_copy(SM[:, 0, :], ints[:, 3, :]).then_inc(mask_step, 1)
            dve.wait_ge(mask_step, 4)
            for l, w in enumerate(MASKED_LEVELS):
                dve.tensor_scalar(mask_work[:, l, :], SM[:, 0, :], float(w), None, ALU.is_ge)
            for t in range(TT):
                last = dve.tensor_copy(same_mask[:, t, :], ident[:, :])
            last.then_inc(mask_step, 1)
            dve.wait_ge(mask_step, 5)
            for l, w in enumerate(MASKED_LEVELS):
                dve.scalar_tensor_tensor(mask_work[:, l, :], SM[:, 0, :], 2.0 * w,
                                         mask_work[:, l, :], ALU.is_lt, ALU.mult)
            first, second = slice(0, CHUNK), slice(CHUNK, P)
            dve.memset(dist[first, CHUNK:P], FAR)
            dve.memset(dist[first, P:P + CHUNK], FAR)
            dve.memset(dist[first, P + 3 * CHUNK:P + 4 * CHUNK], FAR)
            dve.memset(dist[second, P:P + 2 * CHUNK], FAR).then_inc(mask_step, 1)
            dve.wait_ge(mask_step, 6)
            for l, w in enumerate(MASKED_LEVELS):
                _, work_right = halves(mask_work[:, l, :], w)
                _, before_right = halves(SM[:, 4, :], w)
                for t in range(TT):
                    last = dve.tensor_tensor(level_mask[:, l, t, :].rearrange("p (n w) -> p n w", w=w),
                                             work_right, before_right, ALU.mult)
            last.then_inc(masks_made, 1)

            norm_x(0)

            dve.wait_ge(rows_transposed, 1)
            dve.tensor_copy(cols[:, :], bank[0][:, 0:N_SMALL + (1 + CONV) * N_CONV]).then_inc(cols_made, 1)
            dve.wait_ge(cols_made, 1)
            l0, l1 = cols[:, 0:HG_HEADS], cols[:, HG_HEADS:2 * HG_HEADS]
            dve.tensor_scalar(q_gain[:, :], cols[:, 2 * HG_HEADS:2 * HG_HEADS + 1], HEAD_DIM ** -0.5,
                              None, ALU.mult)
            dve.tensor_tensor(lb_t[:, 0, :], l0, l1, ALU.max).then_inc(param_step, 1)
            dve.wait_ge(param_step, 1)
            dve.tensor_tensor(lb_t[:, 1, :], l0, lb_t[:, 0, :], ALU.subtract)
            dve.tensor_tensor(lb_t[:, 2, :], l1, lb_t[:, 0, :], ALU.subtract).then_inc(param_step, 1)
            dve.wait_ge(param_exp, 1)
            dve.tensor_tensor(lb_t[:, 3, :], lb_t[:, 1, :], lb_t[:, 2, :], ALU.add).then_inc(param_step, 1)
            dve.wait_ge(param_step, 3)
            dve.reciprocal(lb_t[:, 0, :], lb_t[:, 3, :]).then_inc(param_step, 1)
            dve.wait_ge(param_step, 4)
            dve.tensor_tensor(lb[:, :], lb_t[:, 1, :], lb_t[:, 0, :], ALU.mult).then_inc(param_step, 1)
            dve.wait_ge(param_step, 5)
            dve.tensor_scalar(one_lb[:, :], lb[:, :], -1.0, 1.0, ALU.mult, ALU.add).then_inc(params_made, 1)
            dve.wait_ge(params_made, 1)

            for i in range(RING):
                make_lo(1, i)

            for half in range(2):
                dve.memset(kz[(1 - half) * HEAD_DIM:(2 - half) * HEAD_DIM, half::2, :], 0.0)\
                    .then_inc(kz_made, 1)
            make_lo(2, 0)
            dve.wait_ge(att_rs, 1)
            dve.scalar_tensor_tensor(QN[:, 0, :], bank[0][:, 0:SEQ], cols[:, K_GAIN:K_GAIN + 1], RS[:, 0:SEQ],
                                     ALU.mult, ALU.mult).then_inc(qk_normed, 1)
            dve.wait_ge(qk_normed, 1)
            for g in range(KV_HEADS):
                for half in range(2):
                    dve.tensor_copy(kz[half * HEAD_DIM:(half + 1) * HEAD_DIM, 2 * g + half, :],
                                    QN[g * HEAD_DIM:(g + 1) * HEAD_DIM, 0, :]).then_inc(kz_made, 1)
            for i in range(1, RING):
                make_lo(2, i)
            dve.wait_ge(kz_made, 6)

            def bias_and_max(g, h):
                n = g * 4 + h
                dve.wait_ge(scores_made, n + 1)
                pr = PR[:, h % 2, :]
                dve.scalar_tensor_tensor(pr, dist[:, :], slopes[:, bass.ds(n, 1)],
                                         bank[4 + h % 2][:, 0:3 * P], ALU.mult, ALU.add).then_inc(biased, 1)
                dve.wait_ge(biased, n + 1)
                dve.tensor_reduce(top[:, h, 0:1], pr[:, 0:P], AX, ALU.max)
                dve.tensor_reduce(top[:, h, 1:2], pr[:, P:3 * P], AX, ALU.max).then_inc(max_made, 1)
                dve.wait_ge(max_made, n + 1)
                dve.tensor_scalar(top[:, h, :], top[:, h, :], sink[:, bass.ds(n, 1)], -1.0,
                                  ALU.max, ALU.mult).then_inc(top_made, 1)

            def attention(g, q_bank, quad):
                make_lo(quad, 0)
                dve.wait_ge(att_rs, g + 2)
                dve.scalar_tensor_tensor(QN[:, :, :].rearrange("p a t -> p (a t)"),
                                         q_bank[:, :], q_gain[:, :],
                                         RS[:, :], ALU.mult, ALU.mult).then_inc(qk_normed, 1)
                make_lo(quad, 1)
                bias_and_max(g, 0)
                bias_and_max(g, 1)
                make_lo(quad, 2)
                bias_and_max(g, 2)
                bias_and_max(g, 3)
                make_lo(quad, 3)
                dve.wait_ge(sink_made, g * 4 + 4)
                dve.tensor_tensor(den[:, :, :], den[:, :, :], exp_sink[:, :, :], ALU.add)\
                    .then_inc(den_summed, 1)
                dve.wait_ge(den_summed, g + 1)
                dve.reciprocal(den[:, :, :], den[:, :, :]).then_inc(den_inverted, 1)
                dve.wait_ge(den_inverted, g + 1)
                dve.wait_ge(pv_made, g * 4 + 4 + FREE)
                dve.tensor_tensor(AO[:, :, :].rearrange("p t (h d) -> p (t h) d", h=4),
                                  bank[7][:, :].rearrange("p (a d) -> p a d", d=HEAD_DIM),
                                  den[:, :, :].rearrange("p t (h a) -> p (t h) a", a=1)
                                  .broadcast_to([P, TT * 4, HEAD_DIM]), ALU.mult).then_inc(att_scaled, 1)
                dve.wait_ge(att_hi, g + 1)
                dve.tensor_tensor(mix[:, bass.ds(g * 2, 2), SEQ:2 * SEQ],
                                  bank[6][:, :].rearrange("p (a t) -> p a t", a=2),
                                  mix[:, bass.ds(g * 2, 2), 0:SEQ].bitcast(F32), ALU.subtract)\
                    .then_inc(att_lo, 1)

            with dve.Fori(0, Q_GROUPS // 2) as i:
                for c in range(2):
                    attention(i * 2 + c, bank[1 - c], i * 2 + c + 3)

            def clamp(n):
                dve.wait_ge(sg_exp, n + 1)
                dve.tensor_scalar(SG[:, :], SG[:, :], EXP_MAX, None, ALU.min).then_inc(sg_clamped, 1)

            def left_exponents(l):
                w = (LEVELS + [P])[l]
                b_left, _ = halves(B[:, :], w)
                r = b_left[:, :, w - 1:w].broadcast_to([P, SEQ // w, w])
                return dve.tensor_tensor(E[:, l, 0, :].rearrange("p (n w) -> p n w", w=w), r, b_left,
                                         ALU.subtract)

            def right_exponents(l):
                w = LEVELS[l]
                b_left, b_right = halves(B[:, :], w)
                r = b_left[:, :, w - 1:w].broadcast_to([P, SEQ // w, w])
                return dve.tensor_tensor(E[:, l, 1, :].rearrange("p (n w) -> p n w", w=w), b_right, r,
                                         ALU.subtract)

            def scale_k(l):
                w = LEVELS[l]
                k_left, _ = halves(K[:, :, :].rearrange("p a t -> p (a t)"), w)
                x_left, _ = halves(XK[:, l, :], w)
                return dve.tensor_tensor(x_left, k_left, E[:, l, 0, :].rearrange("p (n w) -> p n w", w=w),
                                         ALU.mult)

            def scale_q(l):
                w = (LEVELS + [P])[l]
                _, q_right = halves(QE[:, :, :].rearrange("p a t -> p (a t)"), w)
                e = E[:, l, 1, :].rearrange("p (n w) -> p n w", w=w)
                return dve.tensor_tensor(e, q_right, e, ALU.mult)

            def q_slot(j, quad):
                clamp(j * 3)
                make_lo(quad + 1, 0)
                dve.wait_ge(forget_scaled, j * 2 + 2)
                fe = FE[:, :, :].rearrange("p a t -> p (a t)")
                dve.tensor_scalar(fe, fe, FORGET_MIN, None, ALU.max).then_inc(forget_made, 1)
                dve.wait_ge(forget_made, j + 1)
                dve.tensor_scalar(K[:, :, :].rearrange("p a t -> p (a t)"), fe, -1.0, 1.0,
                                  ALU.mult, ALU.add).then_inc(k_made, 1)
                make_lo(quad + 1, 1)
                dve.wait_ge(log_made, j + 1)
                dve.tensor_tensor_scan(B[:, :], tile_start[:, :], LF[:, :], 0.0, ALU.mult, ALU.add)\
                    .then_inc(sum_made, 1)
                make_lo(quad + 1, 2)
                dve.wait_ge(sum_made, j + 1)
                for l in range(4):
                    left_exponents(l)
                    last = right_exponents(l)
                last.then_inc(exponents_made, 1)
                make_lo(quad + 1, 3)
                for l in range(4, NL):
                    left_exponents(l)
                    right_exponents(l)
                left_exponents(NL).then_inc(exponents_made, 1)

            def i_slot(j, quad):
                clamp(j * 3 + 1)
                dve.wait_ge(xk_cleared, 1)
                make_lo(quad + 1, 0)
                dve.wait_ge(decays_made, j * 2 + 1)
                for l in range(4):
                    scale_k(l)
                make_lo(quad + 1, 1)
                dve.wait_ge(sg_made, j * 3 + 2)
                q = QE[:, :, :].rearrange("p a t -> p (a t)")
                dve.tensor_tensor(q, bank_q[:, :], SG[:, :], ALU.mult).then_inc(silu_q, 1)
                dve.wait_ge(decays_made, j * 2 + 2)
                for l in range(4, NL):
                    scale_k(l)
                dve.tensor_tensor(E[:, NL, 0, :].rearrange("p (h t) -> p h t", h=2), K[:, :, 0:P],
                                  E[:, NL, 0, :].rearrange("p (h t) -> p h t", h=2), ALU.mult)
                make_lo(quad + 1, 2)
                dve.wait_ge(silu_q, j + 1)
                for l in range(NL + 1):
                    scale_q(l)
                dve.tensor_tensor(Q1[:, :], q[:, 1::2], FE[:, :, :].rearrange("p a t -> p (a t)")[:, 1::2],
                                  ALU.mult).then_inc(q_scaled, 1)
                make_lo(quad + 1, 3)

            def gather_scores(j, h):
                n = j * 2 + h
                dve.wait_ge(levels_made, n + 1)
                st = ST[:, h, 0:TT, :].rearrange("p t c -> p (t c)")
                banks = bank_scores[h]
                b, at = level_columns(NL - 1)
                _, st_right = halves(st, HALF)
                dve.tensor_copy(st_right, banks[b][:, at:at + P].rearrange("p (t c) -> p t c", t=TT))\
                    .then_inc(st_written, 1)
                dve.tensor_copy(ST[:, h, TT, :], banks[2][:, CROSS])
                for l, w in enumerate(MASKED_LEVELS):
                    b, at = level_columns(l if w > 1 else NL)
                    _, st_right = halves(st, w)
                    dve.wait_ge(st_written, n * (NL + 1) + l + 1)
                    dve.sem_inc(st_turn, 1)
                    dve.copy_predicated(
                        st_right,
                        level_mask[:, l, :, :].rearrange("p t c -> p (t c)").bitcast(I32)
                        .rearrange("p (n w) -> p n w", w=w),
                        banks[b][:, at:at + P].rearrange("p (n w) -> p n w", w=w)).then_inc(st_written, 1)
                dve.wait_ge(st_written, (n + 1) * (NL + 1))
                dve.sem_inc(st_turn, 1)
                dve.copy_predicated(st, same_mask[:, :, :].rearrange("p t c -> p (t c)").bitcast(I32),
                                    banks[2][:, SAME]).then_inc(st_made, 1)

            def g_slot(j, quad):
                make_lo(quad + 1, 0)
                make_lo(quad + 1, 1)
                gather_scores(j, 0)
                make_lo(quad + 1, 2)
                gather_scores(j, 1)
                make_lo(quad + 1, 3)

            def f_slot_of_next(j, quad):
                clamp(j * 3 + 2)
                make_lo(quad + 1, 0)
                dve.wait_ge(sg_made, j * 3 + 3)
                ge = GE[:, :, :].rearrange("p a t -> p (a t)")
                dve.tensor_tensor(ge, bank_g[:, :], SG[:, :], ALU.mult).then_inc(silu_g, 1)
                make_lo(quad + 1, 1)
                dve.wait_ge(o_rs, j + 1)
                dve.tensor_tensor(SQ[:, :], RS[:, :], bank_o[:, :], ALU.mult).then_inc(o_normed, 1)
                dve.wait_ge(o_normed, j + 1 + FREE)
                dve.scalar_tensor_tensor(RS[:, :], SQ[:, :], cols[:, HG_GAIN:HG_GAIN + 1], ge,
                                         ALU.mult, ALU.mult).then_inc(o_gated, 1)
                make_lo(quad + 1, 2)
                make_lo(quad + 1, 3)
                dve.wait_ge(hg_hi, j + 1)
                rows_of = bass.ds(j * 2 + KT // 2, 2)
                dve.tensor_tensor(mix[:, rows_of, SEQ:2 * SEQ],
                                  RS[:, :].rearrange("p (a t) -> p a t", a=2),
                                  mix[:, rows_of, 0:SEQ].bitcast(F32), ALU.subtract).then_inc(hg_lo, 1)

            q_slot(0, Q_F0 + 1)
            with dve.Fori(0, PAIRS - 1) as j:
                i_slot(j, j * 4 + Q_F0 + 2)
                g_slot(j, j * 4 + Q_F0 + 3)
                f_slot_of_next(j, j * 4 + Q_F0 + 4)
                q_slot(j + 1, j * 4 + Q_F0 + 5)
            i_slot(PAIRS - 1, Q_OUT - 2)
            g_slot(PAIRS - 1, Q_OUT - 1)
            f_slot_of_next(PAIRS - 1, Q_OUT)

            def add_to_x(group, units, n):
                dve.wait_ge(units_used, units + RING)
                c = bass.ds(n * GT, GT)
                for t in range(TT):
                    last = dve.tensor_tensor(xt[:, t, c], xt[:, t, c], pair_of(group)[t][:, :], ALU.add)
                last.then_inc(groups_evacuated, 1)

            for n in range(OUT_GROUPS):
                for c in range(QUADS_OUT):
                    quad = Q_OUT + n * QUADS_OUT + c
                    if n and c == 0:
                        add_to_x(G_OUT + n - 1, quad * RING, n - 1)
                    if quad > Q_OUT:
                        for i in range(RING):
                            make_lo(quad + 1, i)
            add_to_x(G_UP - 1, Q_UP * RING, OUT_GROUPS - 1)
            dve.memset(U[:, :, 0:2], 0.0).then_inc(u_cleared, 1)
            norm_x(1)
            for i in range(RING):
                make_lo(Q_UP + 1, i)

            def taps(n, ab, g, quad):
                dst = U[:, :, 2:SEQ + 2]
                evacuate(G_UP + ab, (n + Q_UP + 1) * RING, dst)
                for tap, before, after in ((1, tap2, tap1), (0, tap1, tap0)):
                    for c in range(2):
                        col = g * 2 + ab * (N_CONV // 2) + c + conv_col(tap)
                        dve.wait_ge(before, n * 2 + c + 1)
                        dve.scalar_tensor_tensor(C[:, ab, c, :], U[:, c, tap:tap + SEQ],
                                                 cols[:, bass.ds(col, 1)], C[:, ab, c, :],
                                                 ALU.mult, ALU.add).then_inc(after, 1)
                for i in range(2):
                    make_lo(quad, i)

            def a_work(g, quad):
                taps(g * 2, 0, g, quad)
                for i in range(2, RING):
                    make_lo(quad, i)

            def b_work(g, quad):
                taps(g * 2 + 1, 1, g, quad)
                dve.wait_ge(silu_a, g + 1)
                dve.wait_ge(tap0, g * 4 + 4)
                a = C[:, 0, :, :].rearrange("p c t -> p (c t)")
                b = C[:, 1, :, :].rearrange("p c t -> p (c t)")
                dve.tensor_tensor(b, a, b, ALU.mult).then_inc(ab_made, 1)
                make_lo(quad, 2)
                dve.wait_ge(gated_hi, g + 1)
                dve.tensor_tensor(gated[:, bass.ds(g * 2, 2), SEQ:2 * SEQ], C[:, 1, :, :],
                                  gated[:, bass.ds(g * 2, 2), 0:SEQ].bitcast(F32), ALU.subtract)\
                    .then_inc(gated_lo, 1)
                make_lo(quad, 3)

            with dve.Fori(0, UP_GROUPS - 1) as g:
                a_work(g, g * 2 + Q_UP + 2)
                b_work(g, g * 2 + Q_UP + 3)
            a_work(UP_GROUPS - 1, Q_DOWN)
            b_work(UP_GROUPS - 1, Q_DOWN + 1)
            for n in range(OUT_GROUPS):
                for u in range(n * DOWN_UNITS, (n + 1) * DOWN_UNITS):
                    if u >= 2 * RING:
                        make_lo(Q_DOWN + u // RING, u % RING)
                    if n and u == n * DOWN_UNITS + RING - 1:
                        add_to_x(G_DOWN + n - 1, Q_DOWN * RING + n * DOWN_UNITS, n - 1)
            add_to_x(G_DOWN + OUT_GROUPS - 1, Q_DOWN * RING + OUT_GROUPS * DOWN_UNITS, OUT_GROUPS - 1)

        @block.tensor
        def _(pe):
            def transpose(dst, src, n=P):
                return pe.transpose(dst, src, ident[0:n, 0:n])

            def norm_transposes(which):
                for r in range(TT * KT // 4):
                    t, k = divmod(r, KT // 4)
                    pe.wait_ge(x_normed, which * TT + t + 1)
                    if r >= 4:
                        pe.wait_ge(h_lo, which * TT * KT // 4 + r - 3)
                    for i in range(4):
                        last = transpose(bank[4 + r % 4][:, i * P:(i + 1) * P],
                                         hn[:, t, (4 * k + i) * P:(4 * k + i + 1) * P])
                    last.then_inc(x_transposed, 1)

            def unit_channels(quad, i, group):
                pe.wait_ge(units_split, quad * RING + i + 1 + RING)
                banks = pair_of(group)
                for k in range(4):
                    for b in range(2):
                        c = slice(k * GC + b * P, k * GC + (b + 1) * P)
                        x_k = hs[:, 4 * i + k, :]
                        pe.matmul(banks[b][:, :], w_hi[:, i, c], x_k, start=(i == 0 and k == 0), stop=False)
                        last = pe.matmul(banks[b][:, 0:SEQ], w_lo[:, i, c], x_k[:, 0:SEQ], start=False,
                                         stop=(i == RING - 1 and k == 3))
                last.then_inc(units_used, 1)

            def unit_w_in(quad, i, dst):
                pe.wait_ge(units_split, quad * RING + i + 1 + RING)
                for k in range(4):
                    x_hi, x_lo = hs[:, 4 * i + k, 0:SEQ], hs[:, 4 * i + k, SEQ:2 * SEQ]
                    for b in range(2):
                        c = slice(k * GC + b * P, k * GC + (b + 1) * P)
                        o = dst[:, b * SEQ:(b + 1) * SEQ]
                        pe.matmul(o, w_hi[:, i, c], x_hi, start=(i == 0 and k == 0 and b == 0), stop=False,
                                  skip_group_check=True)
                        pe.matmul(o, w_hi[:, i, c], x_lo, start=False, stop=False, skip_group_check=True)
                        last = pe.matmul(o, w_lo[:, i, c], x_hi, start=False,
                                         stop=(i == RING - 1 and k == 3), skip_group_check=True)
                last.then_inc(units_used, 1)

            def unit_tokens(quad, i, group, src, k0, k_all):
                pe.wait_ge(units_split, quad * RING + i + 1 + RING)
                banks = pair_of(group)
                for k in range(2):
                    hi, lo = w_hi[:, i, k * GT:(k + 1) * GT], w_lo[:, i, k * GT:(k + 1) * GT]
                    for t in range(TT):
                        x_hi = src[:, k0 + k, t * P:(t + 1) * P]
                        x_lo = src[:, k0 + k, SEQ + t * P:SEQ + (t + 1) * P]
                        pe.matmul(banks[t][:, :], x_hi, hi, start=(k0 + k == 0), stop=False)
                        pe.matmul(banks[t][:, :], x_hi, lo, start=False, stop=False)
                        last = pe.matmul(banks[t][:, :], x_lo, hi, start=False, stop=(k0 + k == k_all - 1))
                last.then_inc(units_used, 1)

            pe.wait_ge(pool_done, 1)
            pe.wait_ge(rows_loaded, 16 * (1 + 4 + 1 + 1 + CONV + 1))
            transpose(bank[0][:, 0:N_SMALL], rows[0:N_SMALL, 0, :], N_SMALL)
            for i in range(1 + CONV):
                at = N_SMALL + i * N_CONV
                last = transpose(bank[0][:, at:at + N_CONV], rows[0:N_CONV, 1 + i, :], N_CONV)
            last.then_inc(rows_transposed, 1)
            norm_transposes(0)
            pe.wait_ge(h_lo, TT * KT // 4)
            pe.wait_ge(cols_made, 1)

            for i in range(RING):
                unit_w_in(0, i, bank[0])
            unit_w_in(1, 0, bank[1])
            pe.wait_ge(att_squared, 1)
            pe.matmul(bank[7][:, 0:SEQ], head_mean[:, :], SQ[:, 0:SEQ], start=True, stop=True)\
                .then_inc(att_mean, 1)
            pe.wait_ge(v_copied, 1)
            for t in range(TT):
                last = transpose(bank[6][:, t * P:(t + 1) * P], FE[:, 1, t * P:(t + 1) * P])
            last.then_inc(v_transposed, 1)
            for i in range(1, RING):
                unit_w_in(1, i, bank[1])

            def scores(g, kv, h):
                a, half = divmod(h, 2)
                k = kz[:, bass.ds(kv * 2 + half, 1), :]
                out_b = bank[4 + h % 2]
                pe.matmul(out_b[:, 0:P], QN[:, a, 0:P], k[:, :, 0:P], start=True, stop=True)
                pe.matmul(out_b[:, P:3 * P], QN[:, a, P:2 * P], k, start=True, stop=True)\
                    .then_inc(scores_made, 1)

            def turn_p(g, h):
                n = g * 4 + h
                pe.wait_ge(exp_made, n + 1)
                if h:
                    pe.wait_ge(pt_made, n)
                for i in range(3):
                    last = transpose(bank[6][:, i * P:(i + 1) * P], PR[:, h % 2, i * P:(i + 1) * P])
                last.then_inc(p_transposed, 1)

            def times_v(g, kv, h):
                n = g * 4 + h
                pe.wait_ge(pt_made, n + 1)
                v = [vt[:, t, bass.ds(kv * HEAD_DIM, HEAD_DIM)] for t in range(TT)]
                o = [bank[7][:, (t * 4 + h) * HEAD_DIM:(t * 4 + h + 1) * HEAD_DIM] for t in range(TT)]
                pe.matmul(o[0], PT[:, 0:P], v[0], start=True, stop=True)
                pe.matmul(o[1], PT[:, P:2 * P], v[0], start=True, stop=False)
                pe.matmul(o[1], PT[:, 2 * P:3 * P], v[1], start=False, stop=True).then_inc(pv_made, 1)

            def attention(g, kv, quad, dst):
                pe.wait_ge(qk_normed, g + 1)
                unit_w_in(quad, 0, dst)
                pe.wait_ge(att_squared, g + 2)
                pe.matmul(bank[7][:, :], head_mean[:, :], SQ[:, :], start=True, stop=True)\
                    .then_inc(att_mean, 1)
                unit_w_in(quad, 1, dst)
                pe.wait_ge(qk_normed, g + 2)
                pe.wait_ge(kz_made, 6)
                scores(g, kv, 0)
                scores(g, kv, 1)
                unit_w_in(quad, 2, dst)
                pe.wait_ge(vt_made, 1)
                turn_p(g, 0)
                times_v(g, kv, 0)
                pe.wait_ge(biased, g * 4 + 1)
                scores(g, kv, 2)
                turn_p(g, 1)
                times_v(g, kv, 1)
                pe.wait_ge(biased, g * 4 + 2)
                scores(g, kv, 3)
                unit_w_in(quad, 3, dst)
                turn_p(g, 2)
                times_v(g, kv, 2)
                turn_p(g, 3)
                times_v(g, kv, 3)
                pe.wait_ge(att_scaled, g + 1)
                for a in range(2):
                    for t in range(TT):
                        last = transpose(bank[6][:, (a * TT + t) * P:(a * TT + t + 1) * P],
                                         AO[:, t, a * P:(a + 1) * P])
                last.then_inc(att_transposed, 1)

            with pe.Fori(0, Q_GROUPS // 2) as i:
                for c in range(2):
                    attention(i * 2 + c, i, i * 2 + c + 2, bank[c])

            def q_slot(quad):
                for i in range(RING):
                    unit_w_in(quad, i, bank_q)

            def i_slot(j, quad):
                pe.wait_ge(sg_exp, j * 3 + 1)
                for i in range(RING):
                    unit_w_in(quad, i, bank_i)

            def head_scores(h):
                banks = bank_scores[h]
                for t in range(TT):
                    c = slice(h * SEQ + t * P, h * SEQ + (t + 1) * P)
                    right = slice((h * TT + t) * HALF, (h * TT + t + 1) * HALF)
                    k = K[:, h, t * P:(t + 1) * P]
                    for l in range(NL + 1):
                        b, at = level_columns(l)
                        at += t * HALF
                        pe.matmul(banks[b][:, at:at + HALF], XK[:, l, c] if l < NL else k,
                                  E[:, l, 1, right] if l < NL else Q1[:, right], start=True, stop=True)
                    pe.matmul(banks[2][:, t * P:(t + 1) * P], k, QE[:, h, t * P:(t + 1) * P],
                              start=True, stop=True)
                tile = slice(h * P, (h + 1) * P)
                pe.matmul(banks[2][:, CROSS], E[:, NL, 0, tile], E[:, NL, 1, tile], start=True, stop=True)\
                    .then_inc(levels_made, 1)

            def g_slot(j, quad):
                pe.wait_ge(silu_q, j + 1)
                unit_w_in(quad, 0, bank_g)
                pe.wait_ge(o_normed, j + FREE)
                pe.wait_ge(i_copied, j + 1)
                for h in range(2):
                    for t in range(TT):
                        last = transpose(bank_v[:, (h * TT + t) * P:(h * TT + t + 1) * P],
                                         IE[:, h, t * P:(t + 1) * P])
                last.then_inc(i_transposed, 1)
                unit_w_in(quad, 1, bank_g)
                pe.wait_ge(q_scaled, j + 1)
                head_scores(0)
                unit_w_in(quad, 2, bank_g)
                pe.wait_ge(v_made, j + 1)
                head_scores(1)
                unit_w_in(quad, 3, bank_g)

            def output(j):
                pe.wait_ge(st_made, j * 2 + 2 + FREE)
                for h in range(2):
                    o = h * SEQ
                    pe.matmul(bank_o[:, o:o + P], V[:, h, 0, :], ST[:, h, 0, :], start=True, stop=True)
                    pe.matmul(bank_o[:, o + P:o + SEQ], V[:, h, 0, :], ST[:, h, 2, :], start=True, stop=False)
                    last = pe.matmul(bank_o[:, o + P:o + SEQ], V[:, h, 1, :], ST[:, h, 1, :],
                                     start=False, stop=True)
                last.then_inc(o_made, 1)

            def output_mean(j):
                pe.wait_ge(o_squared, j + 1)
                pe.matmul(bank_mean[:, :], all_mean[:, :], SQ[:, :], start=True, stop=True)\
                    .then_inc(o_mean, 1)

            def f_slot_of_next(j, quad):
                unit_w_in(quad, 0, bank_f)
                output(j)
                unit_w_in(quad, 1, bank_f)
                output_mean(j)
                unit_w_in(quad, 2, bank_f)
                unit_w_in(quad, 3, bank_f)

            pe.wait_ge(qk_normed, 1 + Q_GROUPS)
            q_slot(Q_F0 + 1)
            with pe.Fori(0, PAIRS - 1) as j:
                i_slot(j, j * 4 + Q_F0 + 2)
                g_slot(j, j * 4 + Q_F0 + 3)
                f_slot_of_next(j, j * 4 + Q_F0 + 4)
                pe.wait_ge(silu_g, j + 1)
                q_slot(j * 4 + Q_F0 + 5)
            i_slot(PAIRS - 1, Q_OUT - 2)
            g_slot(PAIRS - 1, Q_OUT - 1)

            pe.wait_ge(att_lo, Q_GROUPS)
            pe.wait_ge(st_made, 2 * PAIRS - 1 + FREE)
            for n in range(OUT_GROUPS):
                pe.wait_ge(groups_evacuated, G_OUT + n + 1)
                for u in range(KT // 2):
                    if n == 0 and 2 * u >= KT // 2:
                        pe.wait_ge(hg_lo, u - KT // 4 + 1)
                    unit_tokens(Q_OUT + n * QUADS_OUT + u // RING, u % RING, G_OUT + n, mix, 2 * u, KT)
                    if n == 0 and u == 0:
                        output(PAIRS - 1)
                    if n == 0 and u == 1:
                        output_mean(PAIRS - 1)

            norm_transposes(1)
            pe.wait_ge(h_lo, 2 * TT * KT // 4)

            with pe.Fori(0, UP_GROUPS) as g:
                for ab in range(2):
                    pe.wait_ge(groups_evacuated, g * 2 + ab + G_UP + 1)
                    for i in range(RING):
                        unit_channels(g * 2 + ab + Q_UP, i, G_UP + ab)

            with pe.Fori(0, OUT_GROUPS // 2) as m:
                for v in range(2 * DOWN_UNITS):
                    n, u = divmod(v, DOWN_UNITS)
                    if u == 0:
                        pe.wait_ge(groups_evacuated, m * 2 + n + G_DOWN + 1)
                    if v == DOWN_UNITS - 1:
                        pe.wait_ge(gated_lo, UP_GROUPS)
                    unit_tokens(m * (2 * DOWN_UNITS // RING) + Q_DOWN + v // RING, v % RING,
                                G_DOWN + n, gated, 2 * u, KT_FF)


_INS = ["x", "attn_norm", "w_in", "q_norm", "k_norm", "attn_sinks", "hg_lb_logits", "hg_norm", "w_out",
        "ffn_norm", "w_ffn_up", "ffn_conv_w", "ffn_conv_b", "w_ffn_down"]
_LAYER = {"w_in", "w_out", "w_ffn_up", "ffn_conv_w", "w_ffn_down"}


def kernel(**inputs):
    import numpy as _np
    import concourse.bacc as _bacc
    from concourse import mybir as _mybir
    from concourse.bass_utils import run_bass_kernel_spmd as _run

    nc = _bacc.Bacc("TRN2", target_bir_lowering=False, num_devices=1)
    arrays, args = {}, []
    for name in _INS:
        a = _np.ascontiguousarray(inputs[name])
        if name in _LAYER or name == "x":
            a = a[0]
        arrays[f"in_{name}_dram"] = a
        args.append(nc.dram_tensor(f"in_{name}_dram", a.shape, _mybir.dt.from_np(a.dtype),
                                   kind="ExternalInput").ap())
    out = nc.dram_tensor("out_dram", (SEQ, D_MODEL), _mybir.dt.float32, kind="ExternalOutput").ap()
    hybrid_layer(nc, *args, out)
    r = _run(nc, [arrays], core_ids=[0])
    return r.results[0]["out_dram"].reshape(1, SEQ, D_MODEL)
```

```python
import concourse.bass as bass
from concourse import mybir
from contextlib import ExitStack

F32 = mybir.dt.float32
F32R = mybir.dt.float32r
I32 = mybir.dt.int32
ACT = mybir.ActivationFunctionType
ALU = mybir.AluOpType
AX = mybir.AxisListType.X

P = 128
D_MODEL, SEQ, CHUNK = 2048, 256, 64
EPS = 1e-6
HEADS, KV_HEADS, HEAD_DIM = 16, 2, 64
HG_HEADS, HG_DIM = 8, 128
D_FF, CONV = 5632, 3
KT = D_MODEL // P
KT_FF = D_FF // P
TT = SEQ // P
RING = 4
FREE = 1
BANK_PAIRS = 2
GC = 256
GT = 512
Q_GROUPS = HEADS * HEAD_DIM // GC
PAIRS = HG_HEADS // 2
COL_Q, COL_KV = 0, HEADS * HEAD_DIM
COL_HQ = COL_KV + 2 * KV_HEADS * HEAD_DIM
COL_HF = COL_HQ + HG_HEADS * HG_DIM
COL_HI = COL_HF + HG_HEADS * HG_DIM
COL_HG = COL_HI + HG_HEADS * HG_DIM
LEVELS = [2, 4, 8, 16, 32, 64]
MASKED_LEVELS = LEVELS[:-1] + [1]
NL = len(LEVELS)
HALF = P // 2
UP_GROUPS = D_FF // GC
OUT_GROUPS = D_MODEL // GT
NORM_ROUNDS = [(0, 0), (1, 0), (0, 1), (1, 1), (2, 0), (2, 1), (3, 0), (3, 1)]
NORM_ROUNDS_OF_UNIT = [3, 4, 6, 8]
Q_F0 = 1 + Q_GROUPS
QUADS_OUT = KT // 8
Q_OUT = Q_F0 + 4 * PAIRS
Q_UP = Q_OUT + QUADS_OUT * OUT_GROUPS
Q_DOWN = Q_UP + 2 * UP_GROUPS
DOWN_UNITS = KT_FF // 2
G_OUT = 0
G_UP = G_OUT + OUT_GROUPS
G_DOWN = G_UP + 2 * UP_GROUPS
KEYS = P + (SEQ - CHUNK)
FAR = -1e34
EXP_MAX = 2.0 ** 62
FORGET_MIN = 2.0 ** -63


def hybrid_layer(nc, x, attn_norm, w_in, q_norm, k_norm, sinks, lb_logits, hg_norm, w_out,
                 ffn_norm, w_up, conv_w, conv_b, w_down, out):
    ctx = ExitStack()
    with ctx:
        def sb(name, shape, dt=F32):
            return ctx.enter_context(nc.sbuf_tensor(name, shape, dt))

        def sem(name):
            return ctx.enter_context(nc.semaphore(name))

        xt = sb("xt", [P, TT, D_MODEL])
        hs = sb("hs", [P, KT, 2 * SEQ], F32R)
        raw = sb("raw", [P, RING, 1024])
        w_hi = sb("w_hi", [P, RING, 1024], F32R)
        w_lo = sb("w_lo", [P, RING, 1024], F32R)
        ident = sb("ident", [P, P])
        head_mean = sb("head_mean", [P, P])
        all_mean = sb("all_mean", [P, P])
        slopes = sb("slopes", [P, HEADS])
        sink = sb("sink", [P, HEADS])
        eps = sb("eps", [P, 1])
        rows = sb("rows", [P, 1 + 1 + CONV, P])
        N_SMALL = 2 * HG_HEADS + 3 + 2 * KT
        N_CONV = 2 * D_FF // P
        cols = sb("cols", [P, N_SMALL + (1 + CONV) * N_CONV])
        lb = sb("lb", [P, HG_HEADS])
        one_lb = sb("one_lb", [P, HG_HEADS])
        lb_t = sb("lb_t", [P, 4, HG_HEADS])
        q_gain = sb("q_gain", [P, 1])
        ss = sb("ss", [P, TT])
        ss_part = sb("ss_part", [P, TT, OUT_GROUPS])
        x_rms_row = sb("x_rms_row", [P, SEQ])
        K_GAIN = 2 * HG_HEADS + 1
        HG_GAIN = 2 * HG_HEADS + 2
        X_GAIN = [2 * HG_HEADS + 3, 2 * HG_HEADS + 3 + KT]
        C_BIAS = N_SMALL

        def conv_col(tap):
            return N_SMALL + (1 + tap) * N_CONV

        def region(name, size):
            sb(name, [P, size // 4])
            return [nc.sbuf_base - size, nc.sbuf_base]

        def sb_at(place, name, shape, dt=F32):
            size = 4
            for n in shape[1:]:
                size *= n
            start = place[0]
            place[0] += size
            place[0] += -place[0] % 32
            assert place[0] <= place[1], name
            return nc.alloc_sbuf_tensor_at(name, shape, dt, offset=start)

        small = region("small_region", 8448)
        place = list(small)
        level_mask = sb_at(place, "level_mask", [P, NL, TT, HALF])
        same_mask = sb_at(place, "same_mask", [P, TT, P])
        tile_start = sb_at(place, "tile_start", [P, 2 * SEQ])
        dist = sb_at(place, "dist", [P, KEYS])
        place = list(small)
        U = sb_at(place, "U", [P, 2, SEQ + 2])
        C = sb_at(place, "C", [P, 2, 2, SEQ])

        large = region("large_region", KT_FF * 2 * SEQ * 4)
        place = list(large)
        mix = sb_at(place, "mix", [P, KT, 2 * SEQ], F32R)
        FE = sb_at(place, "FE", [P, 2, SEQ])
        setup_place = list(place)
        QE = sb_at(place, "QE", [P, 2, SEQ])
        GE = sb_at(place, "GE", [P, 2, SEQ])
        IE = sb_at(place, "IE", [P, 2, SEQ])
        V = sb_at(place, "V", [P, 2, TT, P])
        SG = sb_at(place, "SG", [P, 2 * SEQ])
        SQ = sb_at(place, "SQ", [P, 2 * SEQ])
        RS = sb_at(place, "RS", [P, 2 * SEQ])
        ST = sb_at(place, "ST", [P, 2, 3, P])
        shared = list(place)
        K = sb_at(place, "K", [P, 2, SEQ])
        LF = sb_at(place, "LF", [P, 2 * SEQ])
        B = sb_at(place, "B", [P, 2 * SEQ])
        XK = sb_at(place, "XK", [P, NL, 2 * SEQ])
        Q1 = sb_at(place, "Q1", [P, 2 * SEQ // 2])
        attention_place = list(place)
        E = sb_at(place, "E", [P, NL + 1, 2, 2 * SEQ // 2])
        place = list(setup_place)
        SM = sb_at(place, "SM", [P, 8, P])
        mask_work = sb_at(place, "mask_work", [P, NL, P])
        place = list(attention_place)
        kz = sb_at(place, "kz", [P, KV_HEADS * 2, SEQ])
        vt = sb_at(place, "vt", [P, 3, P])
        QN = sb_at(place, "QN", [P, 2, SEQ])
        PR = sb_at(place, "PR", [P, 4, KEYS])
        PT = sb_at(place, "PT", [P, 2, 3 * P])
        AO = sb_at(place, "AO", [P, TT, 4 * HEAD_DIM])
        top = sb_at(place, "top", [P, 4, TT])
        exp_sink = sb("exp_sink", [P, 2, TT, 4])
        den = sb("den", [P, 2, TT, 4])
        place = list(shared)
        squares = sb_at(place, "squares", [P, TT, D_MODEL])
        rms_diag = sb_at(place, "rms_diag", [P, TT, P])
        place = list(large)
        gated = sb_at(place, "gated", [P, KT_FF, 2 * SEQ], F32R)

        bank = [ctx.enter_context(nc.psum_tensor(f"bank{i}", [P, 512], F32)) for i in range(8)]

        loaded = [sem(f"loaded{i}") for i in range(RING)]
        units_hi = sem("units_hi")
        units_split = sem("units_split")
        units_used = sem("units_used")
        groups_evacuated = sem("groups_evacuated")
        x_loaded = [sem(f"x_loaded{t}") for t in range(TT)]
        small_loaded, conv_loaded = sem("small_loaded"), sem("conv_loaded")
        pool_done, masks_made, cols_made, params_made = (
            sem("pool_done"), sem("masks_made"), sem("cols_made"), sem("params_made"))
        setup_step, mask_step = sem("setup_step"), sem("mask_step")
        param_step, param_exp = sem("param_step"), sem("param_exp")
        rows_transposed, xk_cleared = sem("rows_transposed"), sem("xk_cleared")
        x_scaled = sem("x_scaled")
        x_squared, x_summed, x_rms, x_rs, x_diag, row_spread, row_made = (
            sem("x_squared"), sem("x_summed"), sem("x_rms"), sem("x_rs"), sem("x_diag"),
            sem("row_spread"), sem("row_made"))
        x_transposed, h_hi, h_lo, u_summed = (
            sem("x_transposed"), sem("h_hi"), sem("h_lo"), sem("u_summed"))
        att_squared, att_mean, att_ln, att_rs, qk_normed = (
            sem("att_squared"), sem("att_mean"), sem("att_ln"), sem("att_rs"), sem("qk_normed"))
        kz_made, v_copied, v_transposed, vt_made = (
            sem("kz_made"), sem("v_copied"), sem("v_transposed"), sem("vt_made"))
        scores_made, biased, max_made, top_made = (
            sem("scores_made"), sem("biased"), sem("max_made"), sem("top_made"))
        exp_made, p_transposed, pt_made, pv_made = (
            sem("exp_made"), sem("p_transposed"), sem("pt_made"), sem("pv_made"))
        sink_made, den_summed, den_inverted, att_scaled = (
            sem("sink_made"), sem("den_summed"), sem("den_inverted"), sem("att_scaled"))
        att_transposed, att_hi, att_lo = sem("att_transposed"), sem("att_hi"), sem("att_lo")
        sg_clamped, sg_exp, sg_ln, sg_made = (
            sem("sg_clamped"), sem("sg_exp"), sem("sg_ln"), sem("sg_made"))
        forget_scaled, forget_made, log_made, k_made, sum_made = (
            sem("forget_scaled"), sem("forget_made"), sem("log_made"), sem("k_made"), sem("sum_made"))
        exponents_made, decays_made, k_scaled, silu_q, q_scaled, silu_g = (
            sem("exponents_made"), sem("decays_made"), sem("k_scaled"), sem("silu_q"),
            sem("q_scaled"), sem("silu_g"))
        i_copied, i_transposed, v_made, levels_made, st_written, st_turn, st_made = (
            sem("i_copied"), sem("i_transposed"), sem("v_made"), sem("levels_made"),
            sem("st_written"), sem("st_turn"), sem("st_made"))
        o_made, o_squared, o_mean, o_ln, o_rs = (
            sem("o_made"), sem("o_squared"), sem("o_mean"), sem("o_ln"), sem("o_rs"))
        o_normed, o_gated, hg_hi, hg_lo = sem("o_normed"), sem("o_gated"), sem("hg_hi"), sem("hg_lo")
        u_cleared, tap2, tap1, tap0 = sem("u_cleared"), sem("tap2"), sem("tap1"), sem("tap0")
        silu_a, ab_made, gated_hi, gated_lo = (
            sem("silu_a"), sem("ab_made"), sem("gated_hi"), sem("gated_lo"))
        first_tile_done = sem("first_tile_done")
        last_added = sem("last_added")
        stored = sem("stored")

        w_in_v = w_in.rearrange("(k p) n -> p k n", p=P)
        w_out_v = w_out.rearrange("(k p) n -> p k n", p=P)
        w_up_v = w_up.rearrange("(k p) n -> p k n", p=P)
        w_down_v = w_down.rearrange("(k p) n -> p k n", p=P)
        x_v = x.rearrange("(t p) n -> p t n", p=P)
        out_v = out.rearrange("(t p) n -> p t n", p=P)

        def pair_of(group):
            b = 2 * ((group + 1) % BANK_PAIRS)
            return bank[b], bank[b + 1]

        bank_s, bank_p, bank_pv, bank_m, bank_ao = bank[2:4], bank[4:6], bank[6], bank[7], bank[7]
        bank_f = bank_i = bank[1]
        bank_q = bank_g = bank[0]
        bank_scores = [bank[2:5], bank[5:8]]
        bank_o, bank_mean, bank_v = bank[6], bank[7], bank[7]
        SAME, CROSS = slice(0, 2 * P), slice(2 * P, 3 * P)

        def level_columns(l):
            return l // 4, (l % 4) * P

        def halves(ap, width):
            v = ap.rearrange("p (n two w) -> p n two w", two=2, w=width)
            return v[:, :, 0, :], v[:, :, 1, :]

        block = ctx.enter_context(nc.Block())

        @block.sync
        def _(sp):
            for t in range(TT):
                sp.dma_start(xt[:, t, :], x_v[:, t, :]).then_inc(x_loaded[t], 16)
            for i, g in enumerate((attn_norm, ffn_norm)):
                sp.dma_start(rows[X_GAIN[i]:X_GAIN[i] + KT, 0, :], g.rearrange("a (r c) -> (a r) c", c=P))\
                    .then_inc(small_loaded, 16)
            sp.dma_start(rows[0:2 * HG_HEADS, 0, :], lb_logits.rearrange("l (h c) -> (l h) c", c=P))\
                .then_inc(small_loaded, 16)
            for i in range(2):
                c = slice(i * HEAD_DIM, (i + 1) * HEAD_DIM)
                sp.dma_start(rows[2 * HG_HEADS:2 * HG_HEADS + 1, 0, c], q_norm).then_inc(small_loaded, 16)
                sp.dma_start(rows[K_GAIN:K_GAIN + 1, 0, c], k_norm).then_inc(small_loaded, 16)
            sp.dma_start(rows[HG_GAIN:HG_GAIN + 1, 0, :], hg_norm).then_inc(small_loaded, 16)

            def load_unit(quad, i, view, row, rows_n, col, cols_n):
                sp.wait_ge(units_split, quad * RING + i + 1)
                sp.dma_start(raw[:, i, :].rearrange("p (k n) -> p k n", k=rows_n),
                             view[:, row:row + rows_n, bass.ds(col, cols_n)]).then_inc(loaded[i], 16)

            def load_channels(quad, view, col):
                for i in range(RING):
                    load_unit(quad, i, view, 4 * i, 4, col, GC)

            load_channels(0, w_in_v, COL_KV)
            sp.dma_start(rows[0:N_CONV, 1, :], conv_b.rearrange("a (r c) -> (a r) c", c=P))\
                .then_inc(conv_loaded, 16)
            for tap in range(CONV):
                sp.dma_start(rows[0:N_CONV, 2 + tap, :],
                             conv_w[tap:tap + 1, :].rearrange("a (r c) -> (a r) c", c=P))\
                    .then_inc(conv_loaded, 16)
            sp.dma_start(sink[:, :], sinks.broadcast_to([P, HEADS])).then_inc(conv_loaded, 16)
            with sp.Fori(0, Q_GROUPS) as g:
                load_channels(g + 1, w_in_v, g * GC + COL_Q)
            load_channels(Q_F0, w_in_v, COL_HF)
            load_channels(Q_F0 + 1, w_in_v, COL_HQ)
            with sp.Fori(0, PAIRS - 1) as j:
                load_channels(j * 4 + Q_F0 + 2, w_in_v, j * GC + COL_HI)
                load_channels(j * 4 + Q_F0 + 3, w_in_v, j * GC + COL_HG)
                load_channels(j * 4 + Q_F0 + 4, w_in_v, j * GC + COL_HF + GC)
                load_channels(j * 4 + Q_F0 + 5, w_in_v, j * GC + COL_HQ + GC)
            load_channels(Q_OUT - 2, w_in_v, COL_HI + (PAIRS - 1) * GC)
            load_channels(Q_OUT - 1, w_in_v, COL_HG + (PAIRS - 1) * GC)
            with sp.Fori(0, OUT_GROUPS) as n:
                for c in range(QUADS_OUT):
                    for i in range(RING):
                        load_unit(n * QUADS_OUT + Q_OUT + c, i, w_out_v, 8 * c + 2 * i, 2, n * GT, GT)
            with sp.Fori(0, UP_GROUPS) as g:
                load_channels(g * 2 + Q_UP, w_up_v, g * GC)
                load_channels(g * 2 + Q_UP + 1, w_up_v, g * GC + D_FF)
            with sp.Fori(0, OUT_GROUPS // 2) as m:
                for v in range(2 * DOWN_UNITS):
                    n, u = divmod(v, DOWN_UNITS)
                    load_unit(m * (2 * DOWN_UNITS // RING) + Q_DOWN + v // RING, v % RING,
                              w_down_v, 2 * u, 2, m * (2 * GT) + n * GT, GT)

        @block.gpsimd
        def _(pool):
            pool.sem_inc(units_split, RING)
            pool.sem_inc(units_used, RING)
            pool.sem_inc(groups_evacuated, BANK_PAIRS)
            for s in (st_made, o_normed, ab_made):
                pool.sem_inc(s, FREE)
            pool.memset(ident[:, :], 0.0).then_inc(setup_step, 1)
            pool.memset(all_mean[:, :], 1.0 / HG_DIM)
            pool.memset(eps[:, :], EPS)
            for h in range(HEADS):
                pool.memset(slopes[:, h:h + 1], 2.0 ** (-8.0 * (h + 1) / HEADS))
            pool.memset(tile_start[:, :], 1.0).then_inc(setup_step, 1)
            ints = SM[:, :, :].bitcast(I32)
            pool.iota(ints[:, 0, :], [[0, P]], base=0, channel_multiplier=1)
            pool.iota(ints[:, 1, :], [[1, P]], base=0, channel_multiplier=0)
            pool.iota(ints[:, 2, :], [[1, P]], base=0, channel_multiplier=-1)
            pool.iota(ints[:, 5, :], [[-1, P]], base=0, channel_multiplier=1)
            pool.iota(ints[:, 6:8, :].rearrange("p a b -> p (a b)"), [[-1, 2 * P]], base=P - CHUNK,
                      channel_multiplier=1)
            pool.wait_ge(setup_step, 2)
            pool.affine_select(out=ident[:, :], in_=ident[:, :], compare_op=ALU.not_equal, fill=1.0,
                               base=0, pattern=[[-1, P]], channel_multiplier=1)
            pool.memset(tile_start[:, :].rearrange("p (n w) -> p n w", w=P)[:, :, 0:1], 0.0)\
                .then_inc(pool_done, 1)
            pool.memset(ST[:, :, :, :], 0.0)
            pool.wait_ge(x_transposed, 2 * KT // 4)
            pool.memset(XK[:, :, :], 0.0).then_inc(xk_cleared, 1)

        @block.scalar
        def _(act):
            act.preload_act_table_set("natural_log_exp_and_others")
            act.wait_ge(pool_done, 1)

            def make_hi(quad, i):
                act.wait_ge(loaded[i], quad * 16 + 16)
                act.wait_ge(units_used, quad * RING + i + 1)
                act.copy(w_hi[:, i, :], raw[:, i, :]).then_inc(units_hi, 1)

            def inverse_rms(t, n):
                act.activation(ss[:, t:t + 1], ss[:, t:t + 1], ACT.Ln, scale=1.0 / D_MODEL,
                               bias=eps[:, :]).then_inc(x_rms, 1)
                act.wait_ge(x_rms, n + 1)
                act.activation(ss[:, t:t + 1], ss[:, t:t + 1], ACT.Exp, scale=-0.5).then_inc(x_rs, 1)

            def rms_on_diagonal(t):
                act.wait_ge(x_rs, TT + t + 1)
                act.activation(rms_diag[:, t, :], ident[:, :], ACT.Identity, scale=ss[:, t:t + 1])\
                    .then_inc(x_diag, 1)

            def h_hi_round(which, k, t, n, out_b):
                act.wait_ge(x_transposed, n + 1)
                for i in range(4):
                    col = X_GAIN[which] + 4 * k + i
                    last = act.activation(hs[:, 4 * k + i, t * P:(t + 1) * P], out_b[:, i * P:(i + 1) * P],
                                          ACT.Identity, scale=cols[:, col:col + 1])
                last.then_inc(h_hi, 1)

            for t in range(TT):
                act.wait_ge(x_loaded[t], 16)
                act.activation(squares[:, t, :], xt[:, t, :], ACT.Square, accum_out=ss[:, t:t + 1])\
                    .then_inc(x_squared, 1)
                act.wait_ge(x_squared, t + 1)
                inverse_rms(t, t)
            act.wait_ge(cols_made, 1)
            for n, (k, t) in enumerate(NORM_ROUNDS):
                h_hi_round(0, k, t, n, bank[4 + n % 4])
                if n + 1 in NORM_ROUNDS_OF_UNIT:
                    make_hi(0, NORM_ROUNDS_OF_UNIT.index(n + 1))
            for i in range(RING):
                make_hi(1, i)
                if i == 0:
                    act.wait_ge(param_step, 2)
                    act.activation(lb_t[:, 1:3, :], lb_t[:, 1:3, :], ACT.Exp).then_inc(param_exp, 1)

            def att_rms(a, width):
                act.wait_ge(att_mean, a + 1)
                act.activation(RS[:, 0:width], bank[7][:, 0:width], ACT.Ln, bias=eps[:, :])\
                    .then_inc(att_ln, 1)
                act.wait_ge(att_ln, a + 1)
                act.activation(RS[:, 0:width], RS[:, 0:width], ACT.Exp, scale=-0.5).then_inc(att_rs, 1)

            act.wait_ge(units_used, 2 * RING)
            act.activation(SQ[:, 0:SEQ], bank[0][:, 0:SEQ], ACT.Square).then_inc(att_squared, 1)
            act.copy(FE[:, 1, :], bank[0][:, SEQ:2 * SEQ]).then_inc(v_copied, 1)
            make_hi(2, 0)
            att_rms(0, SEQ)
            act.wait_ge(v_transposed, 1)
            act.copy(vt[:, 0:2, :].rearrange("p t c -> p (t c)"), bank_p[0][:, 0:2 * P])
            act.copy(vt[0:CHUNK, 2, :], bank_p[0][0:CHUNK, 2 * P:3 * P]).then_inc(vt_made, 1)
            for i in range(1, RING):
                make_hi(2, i)

            def exponentials(g, h):
                n = g * 4 + h
                act.wait_ge(top_made, n + 1)
                if g >= 2:
                    act.wait_ge(att_scaled, g - 1)
                act.activation(PR[:, h, 0:P], PR[:, h, 0:P], ACT.Exp, bias=top[:, h, 0:1],
                               accum_out=den[:, g % 2, 0, h:h + 1])
                act.activation(PR[:, h, P:KEYS], PR[:, h, P:KEYS], ACT.Exp, bias=top[:, h, 1:2],
                               accum_out=den[:, g % 2, 1, h:h + 1]).then_inc(exp_made, 1)
                act.activation(exp_sink[:, g % 2, :, h], top[:, h, :], ACT.Exp, bias=sink[:, n:n + 1])\
                    .then_inc(sink_made, 1)

            def copy_pt(g, h):
                n = g * 4 + h
                act.wait_ge(p_transposed, n + 1)
                if n >= 2:
                    act.wait_ge(pv_made, n - 1)
                act.copy(PT[:, h % 2, 0:2 * P], bank_p[h % 2][:, 0:2 * P])
                act.copy(PT[0:CHUNK, h % 2, 2 * P:3 * P], bank_p[h % 2][0:CHUNK, 2 * P:3 * P])\
                    .then_inc(pt_made, 1)

            def att_mix_hi(g):
                act.wait_ge(att_transposed, g + 1)
                act.copy(mix[:, 2 * g:2 * g + 2, 0:SEQ], bank_ao[:, :].rearrange("p (a t) -> p a t", a=2))\
                    .then_inc(att_hi, 1)

            def attention(g, quad):
                act.wait_ge(units_used, (quad + 1) * RING)
                act.activation(SQ[:, :], bank[(quad - 1) % 2][:, :], ACT.Square).then_inc(att_squared, 1)
                if g:
                    copy_pt(g - 1, 2)
                make_hi(quad + 1, 0)
                if g:
                    copy_pt(g - 1, 3)
                att_rms(g + 1, 2 * SEQ)
                make_hi(quad + 1, 1)
                exponentials(g, 0)
                exponentials(g, 1)
                if g:
                    att_mix_hi(g - 1)
                copy_pt(g, 0)
                make_hi(quad + 1, 2)
                exponentials(g, 2)
                copy_pt(g, 1)
                make_hi(quad + 1, 3)
                exponentials(g, 3)

            for g in range(Q_GROUPS):
                attention(g, g + 2)

            def sigmoid_exp(n, src, quad):
                act.wait_ge(units_used, (quad + 2) * RING)
                act.activation(SG[:, :], src[:, :], ACT.Exp, scale=-1.0).then_inc(sg_exp, 1)

            def sigmoid_rest(n):
                act.wait_ge(sg_clamped, n + 1)
                act.activation(SG[:, :], SG[:, :], ACT.Ln, bias=1.0).then_inc(sg_ln, 1)
                act.wait_ge(sg_ln, n + 1)
                act.activation(SG[:, :], SG[:, :], ACT.Exp, scale=-1.0).then_inc(sg_made, 1)


            def q_slot(j, quad, attention_ends=False):
                sigmoid_exp(j * 3, bank_f, quad - 1)
                if attention_ends:
                    copy_pt(Q_GROUPS - 1, 2)
                make_hi(quad + 1, 0)
                if attention_ends:
                    copy_pt(Q_GROUPS - 1, 3)
                sigmoid_rest(j * 3)
                act.wait_ge(sg_made, j * 3 + 1)
                for h in range(2):
                    act.activation(FE[:, h, :], SG[:, h * SEQ:(h + 1) * SEQ], ACT.Identity,
                                   scale=one_lb[:, bass.ds(j * 2 + h, 1)],
                                   bias=lb[:, bass.ds(j * 2 + h, 1)]).then_inc(forget_scaled, 1)
                make_hi(quad + 1, 1)
                if attention_ends:
                    att_mix_hi(Q_GROUPS - 1)
                act.wait_ge(forget_made, j + 1)
                act.activation(LF[:, :], FE[:, :, :].rearrange("p a t -> p (a t)"), ACT.Ln)\
                    .then_inc(log_made, 1)
                make_hi(quad + 1, 2)
                make_hi(quad + 1, 3)
                act.wait_ge(exponents_made, j * 2 + 1)
                e = E[:, 0:4, :, :]
                act.activation(e, e, ACT.Exp).then_inc(decays_made, 1)

            def i_slot(j, quad):
                sigmoid_exp(j * 3 + 1, bank_q, quad - 1)
                make_hi(quad + 1, 0)
                act.wait_ge(exponents_made, j * 2 + 2)
                act.activation(E[:, NL, 1, :].rearrange("p (h t) -> p h t", h=2),
                               halves(B[:, :], P)[1], ACT.Exp)
                act.activation(E[:, 4:NL, :, :], E[:, 4:NL, :, :], ACT.Exp)
                act.activation(E[:, NL, 0, :], E[:, NL, 0, :], ACT.Exp).then_inc(decays_made, 1)
                sigmoid_rest(j * 3 + 1)
                for i in range(1, RING):
                    make_hi(quad + 1, i)

            def g_slot(j, quad):
                act.wait_ge(units_used, (quad + 1) * RING)
                act.copy(IE[:, :, :].rearrange("p a t -> p (a t)"), bank_i[:, :]).then_inc(i_copied, 1)
                make_hi(quad + 1, 0)
                make_hi(quad + 1, 1)
                act.wait_ge(i_transposed, j + 1)
                act.copy(V[:, :, :, :].rearrange("p h t c -> p (h t c)"), bank_v[:, :]).then_inc(v_made, 1)
                make_hi(quad + 1, 2)
                make_hi(quad + 1, 3)

            def f_slot_of_next(j, quad):
                sigmoid_exp(j * 3 + 2, bank_g, quad - 1)
                make_hi(quad + 1, 0)
                sigmoid_rest(j * 3 + 2)
                act.wait_ge(o_made, j + 1)
                act.activation(SQ[:, :], bank_o[:, :], ACT.Square).then_inc(o_squared, 1)
                make_hi(quad + 1, 1)
                act.wait_ge(o_mean, j + 1)
                act.activation(RS[:, :], bank_mean[:, :], ACT.Ln, bias=eps[:, :]).then_inc(o_ln, 1)
                act.wait_ge(o_ln, j + 1)
                act.activation(RS[:, :], RS[:, :], ACT.Exp, scale=-0.5).then_inc(o_rs, 1)
                make_hi(quad + 1, 2)
                make_hi(quad + 1, 3)
                act.wait_ge(o_gated, j + 1)
                act.copy(mix[:, bass.ds(j * 2 + KT // 2, 2), 0:SEQ],
                         RS[:, :].rearrange("p (a t) -> p a t", a=2)).then_inc(hg_hi, 1)

            q_slot(0, Q_F0 + 1, attention_ends=True)
            with act.Fori(0, PAIRS - 1) as j:
                i_slot(j, j * 4 + Q_F0 + 2)
                g_slot(j, j * 4 + Q_F0 + 3)
                f_slot_of_next(j, j * 4 + Q_F0 + 4)
                q_slot(j + 1, j * 4 + Q_F0 + 5)
            i_slot(PAIRS - 1, Q_OUT - 2)
            g_slot(PAIRS - 1, Q_OUT - 1)
            f_slot_of_next(PAIRS - 1, Q_OUT)

            def second_norm(n):
                act.wait_ge(groups_evacuated, G_OUT + n + 1 + BANK_PAIRS)
                c = slice(n * GT, (n + 1) * GT)
                for t in range(TT):
                    act.activation(squares[:, t, c], xt[:, t, c], ACT.Square,
                                   accum_out=ss_part[:, t, n:n + 1]).then_inc(x_squared, 1)
                for t in range(TT):
                    h_hi_round(1, n, t, (KT // 4 + n) * TT + t, bank[4 + t])

            for i in range(RING):
                make_hi(Q_OUT + 2, i)
            for n in range(1, OUT_GROUPS):
                make_hi(Q_OUT + 2 * n + 1, 0)
                second_norm(n - 1)
                for i in range(1, RING):
                    make_hi(Q_OUT + 2 * n + 1, i)
                for i in range(RING):
                    make_hi(Q_OUT + 2 * n + 2, i)
            make_hi(Q_UP + 1, 0)
            second_norm(OUT_GROUPS - 1)
            make_hi(Q_UP + 1, 1)
            act.wait_ge(x_summed, 1)
            for t in range(TT):
                inverse_rms(t, TT + t)
                rms_on_diagonal(t)
            act.preload_act_table_set("silu_and_others")
            make_hi(Q_UP + 1, 2)
            act.wait_ge(row_spread, 1)
            act.activation(x_rms_row[:, :], bank[6][:, 0:SEQ], ACT.Identity, scale=float(HG_DIM))\
                .then_inc(row_made, 1)
            make_hi(Q_UP + 1, 3)

            def last_tap(n, ab, g):
                act.wait_ge(groups_evacuated, n + BANK_PAIRS + G_UP + 1)
                for c in range(2):
                    col = g * 2 + ab * (N_CONV // 2) + c
                    act.activation(C[:, ab, c, :], U[:, c, 2:SEQ + 2], ACT.Identity,
                                   scale=cols[:, bass.ds(col + conv_col(2), 1)],
                                   bias=cols[:, bass.ds(col + C_BIAS, 1)]).then_inc(tap2, 1)

            def a_work(g, quad):
                make_hi(quad, 0)
                act.wait_ge(ab_made, g + FREE)
                last_tap(g * 2, 0, g)
                make_hi(quad, 1)
                act.wait_ge(tap0, g * 4 + 2)
                a = C[:, 0, :, :].rearrange("p c t -> p (c t)")
                act.activation(a, a, ACT.Silu).then_inc(silu_a, 1)
                for i in range(2, RING):
                    make_hi(quad, i)

            def b_work(g, quad):
                make_hi(quad, 0)
                last_tap(g * 2 + 1, 1, g)
                make_hi(quad, 1)
                make_hi(quad, 2)
                act.wait_ge(ab_made, g + 1 + FREE)
                act.copy(gated[:, bass.ds(g * 2, 2), 0:SEQ], C[:, 1, :, :]).then_inc(gated_hi, 1)
                make_hi(quad, 3)

            with act.Fori(0, UP_GROUPS - 1) as g:
                a_work(g, g * 2 + Q_UP + 2)
                b_work(g, g * 2 + Q_UP + 3)
            a_work(UP_GROUPS - 1, Q_DOWN)
            b_work(UP_GROUPS - 1, Q_DOWN + 1)

            def store(n):
                act.wait_ge(groups_evacuated, n + BANK_PAIRS + G_DOWN + 1)
                act.dma_start(out_v[:, :, bass.ds(n * GT, GT)], xt[:, :, bass.ds(n * GT, GT)])\
                    .then_inc(stored, 16)

            for n in range(OUT_GROUPS):
                for u in range(n * DOWN_UNITS, (n + 1) * DOWN_UNITS):
                    if u >= 2 * RING:
                        make_hi(Q_DOWN + u // RING, u % RING)
                    if n and u == n * DOWN_UNITS + 2 * RING:
                        store(n - 1)
            c = slice((OUT_GROUPS - 1) * GT, OUT_GROUPS * GT)
            for t in range(TT):
                act.wait_ge(last_added, t + 1)
                act.dma_start(out_v[:, t, c], xt[:, t, c]).then_inc(stored, 16)
            act.wait_ge(stored, 16 * (OUT_GROUPS - 1 + TT))

        @block.vector
        def _(dve):
            def make_lo(quad, i):
                dve.wait_ge(units_hi, quad * RING + i + 1)
                dve.tensor_tensor(w_lo[:, i, :], raw[:, i, :], w_hi[:, i, :].bitcast(F32), ALU.subtract)\
                    .then_inc(units_split, 1)

            def evacuate(group, n, units, dst):
                dve.wait_ge(units_used, units + RING)
                b0, b1 = pair_of(group)
                dve.tensor_reduce(dst[:, 0, :], b0[:, :].rearrange("p (h t) -> p t h", h=2), AX, ALU.add)
                dve.tensor_reduce(dst[:, 1, :], b1[:, :].rearrange("p (h t) -> p t h", h=2), AX, ALU.add)\
                    .then_inc(u_summed, 1)
                dve.wait_ge(u_summed, n + 1)
                dve.tensor_tensor(dst, dst, x_rms_row[:, :].rearrange("p (c t) -> p c t", c=1)
                                  .broadcast_to([P, 2, SEQ]), ALU.mult).then_inc(groups_evacuated, 1)

            def h_lo_round(which, k, t, n, out_b):
                dve.wait_ge(h_hi, n + 1)
                for i in range(4):
                    col = X_GAIN[which] + 4 * k + i
                    tokens = slice(t * P, (t + 1) * P)
                    last = dve.scalar_tensor_tensor(hs[:, 4 * k + i, SEQ + t * P:SEQ + (t + 1) * P],
                                                    out_b[:, i * P:(i + 1) * P], cols[:, col:col + 1],
                                                    hs[:, 4 * k + i, tokens].bitcast(F32),
                                                    ALU.mult, ALU.subtract)
                last.then_inc(h_lo, 1)

            dve.memset(head_mean[:, :], 0.0).then_inc(mask_step, 1)
            dve.wait_ge(mask_step, 1)
            for h in range(2):
                s = slice(h * HEAD_DIM, (h + 1) * HEAD_DIM)
                dve.memset(head_mean[s, s], 1.0 / HEAD_DIM)
            for t in range(TT):
                dve.wait_ge(x_rs, t + 1)
                for k in range(KT // 4):
                    c = slice(k * GT, (k + 1) * GT)
                    dve.tensor_scalar(squares[:, t, c], xt[:, t, c], ss[:, t:t + 1], None, ALU.mult)\
                        .then_inc(x_scaled, 1)
                if t == 0:
                    dve.wait_ge(rows_transposed, 1)
                    dve.tensor_copy(cols[:, 0:N_SMALL], bank[3][:, 0:N_SMALL]).then_inc(cols_made, 1)
            dve.wait_ge(cols_made, 1)
            for n, (k, t) in enumerate(NORM_ROUNDS):
                h_lo_round(0, k, t, n, bank[4 + n % 4])
                if n + 1 in NORM_ROUNDS_OF_UNIT:
                    make_lo(0, NORM_ROUNDS_OF_UNIT.index(n + 1))
            make_lo(1, 0)
            dve.wait_ge(rows_transposed, 2)
            dve.tensor_copy(cols[:, N_SMALL:], bank[3][:, N_SMALL:N_SMALL + (1 + CONV) * N_CONV])\
                .then_inc(cols_made, 1)
            l0, l1 = cols[:, 0:HG_HEADS], cols[:, HG_HEADS:2 * HG_HEADS]
            dve.tensor_scalar(q_gain[:, :], cols[:, 2 * HG_HEADS:2 * HG_HEADS + 1], HEAD_DIM ** -0.5,
                              None, ALU.mult)
            dve.tensor_tensor(lb_t[:, 0, :], l0, l1, ALU.max).then_inc(param_step, 1)
            dve.wait_ge(param_step, 1)
            dve.tensor_tensor(lb_t[:, 1, :], l0, lb_t[:, 0, :], ALU.subtract)
            dve.tensor_tensor(lb_t[:, 2, :], l1, lb_t[:, 0, :], ALU.subtract).then_inc(param_step, 1)
            dve.wait_ge(param_exp, 1)
            dve.tensor_tensor(lb_t[:, 3, :], lb_t[:, 1, :], lb_t[:, 2, :], ALU.add).then_inc(param_step, 1)
            dve.wait_ge(param_step, 3)
            dve.reciprocal(lb_t[:, 0, :], lb_t[:, 3, :]).then_inc(param_step, 1)
            dve.wait_ge(param_step, 4)
            dve.tensor_tensor(lb[:, :], lb_t[:, 1, :], lb_t[:, 0, :], ALU.mult).then_inc(param_step, 1)
            dve.wait_ge(param_step, 5)
            dve.tensor_scalar(one_lb[:, :], lb[:, :], -1.0, 1.0, ALU.mult, ALU.add).then_inc(params_made, 1)
            dve.wait_ge(params_made, 1)

            for i in range(1, RING):
                make_lo(1, i)

            dve.wait_ge(pool_done, 1)
            ints = SM[:, :, :].bitcast(I32)
            dve.tensor_tensor(ints[:, 3, :], ints[:, 0, :], ints[:, 1, :], ALU.bitwise_xor)\
                .then_inc(mask_step, 1)
            apart = ints[:, 5:8, :].rearrange("p a b -> p (a b)")[:, 0:KEYS]
            dve.scalar_tensor_tensor(dist[:, :], apart, -1.0, apart, ALU.mult, ALU.min)\
                .then_inc(mask_step, 1)
            dve.tensor_scalar(SM[:, 4, :], ints[:, 2, :], 0.0, None, ALU.is_gt)
            dve.wait_ge(mask_step, 2)
            dve.tensor_copy(SM[:, 0, :], ints[:, 3, :]).then_inc(mask_step, 1)
            dve.wait_ge(mask_step, 4)
            for l, w in enumerate(MASKED_LEVELS):
                dve.tensor_scalar(mask_work[:, l, :], SM[:, 0, :], float(w), None, ALU.is_ge)
            for t in range(TT):
                last = dve.tensor_copy(same_mask[:, t, :], ident[:, :])
            last.then_inc(mask_step, 1)
            dve.wait_ge(mask_step, 5)
            for l, w in enumerate(MASKED_LEVELS):
                dve.scalar_tensor_tensor(mask_work[:, l, :], SM[:, 0, :], 2.0 * w,
                                         mask_work[:, l, :], ALU.is_lt, ALU.mult)
            first, second = slice(0, CHUNK), slice(CHUNK, P)
            dve.memset(dist[first, CHUNK:P], FAR)
            dve.memset(dist[first, P + 2 * CHUNK:P + 3 * CHUNK], FAR)
            dve.memset(dist[second, P:P + CHUNK], FAR).then_inc(mask_step, 1)
            dve.wait_ge(mask_step, 6)
            for l, w in enumerate(MASKED_LEVELS):
                _, work_right = halves(mask_work[:, l, :], w)
                _, before_right = halves(SM[:, 4, :], w)
                for t in range(TT):
                    last = dve.tensor_tensor(level_mask[:, l, t, :].rearrange("p (n w) -> p n w", w=w),
                                             work_right, before_right, ALU.mult)
            last.then_inc(masks_made, 1)

            for half in range(2):
                dve.memset(kz[(1 - half) * HEAD_DIM:(2 - half) * HEAD_DIM, half::2, :], 0.0)\
                    .then_inc(kz_made, 1)
            make_lo(2, 0)
            dve.wait_ge(att_rs, 1)
            dve.scalar_tensor_tensor(QN[:, 0, :], bank[0][:, 0:SEQ], cols[:, K_GAIN:K_GAIN + 1], RS[:, 0:SEQ],
                                     ALU.mult, ALU.mult).then_inc(qk_normed, 1)
            dve.wait_ge(qk_normed, 1)
            for g in range(KV_HEADS):
                for half in range(2):
                    dve.tensor_copy(kz[half * HEAD_DIM:(half + 1) * HEAD_DIM, 2 * g + half, :],
                                    QN[g * HEAD_DIM:(g + 1) * HEAD_DIM, 0, :]).then_inc(kz_made, 1)
            for i in range(1, RING):
                make_lo(2, i)
            dve.wait_ge(kz_made, 6)

            def bias_and_max(g, h):
                n = g * 4 + h
                dve.wait_ge(scores_made, n + 1)
                if g:
                    dve.wait_ge(p_transposed, n - 3)
                dve.scalar_tensor_tensor(PR[:, h, :], dist[:, :], slopes[:, n:n + 1],
                                         bank_s[h % 2][:, 0:KEYS], ALU.mult, ALU.add).then_inc(biased, 1)
                dve.wait_ge(biased, n + 1)
                if g:
                    dve.wait_ge(sink_made, n - 3)
                dve.tensor_reduce(top[:, h, 0:1], PR[:, h, 0:P], AX, ALU.max)
                dve.tensor_reduce(top[:, h, 1:2], PR[:, h, P:KEYS], AX, ALU.max).then_inc(max_made, 1)
                dve.wait_ge(max_made, n + 1)
                dve.tensor_scalar(top[:, h, :], top[:, h, :], sink[:, n:n + 1], -1.0,
                                  ALU.max, ALU.mult).then_inc(top_made, 1)

            def invert_sums(g):
                d = den[:, g % 2, :, :]
                dve.wait_ge(sink_made, g * 4 + 4)
                dve.tensor_tensor(d, d, exp_sink[:, g % 2, :, :], ALU.add).then_inc(den_summed, 1)
                dve.wait_ge(den_summed, g + 1)
                dve.reciprocal(d, d).then_inc(den_inverted, 1)

            def scale_output(g):
                dve.wait_ge(den_inverted, g + 1)
                dve.wait_ge(pv_made, g * 4 + 4)
                dve.tensor_tensor(AO[:, :, :].rearrange("p t (h d) -> p (t h) d", h=4),
                                  bank_pv[:, :].rearrange("p (a d) -> p a d", d=HEAD_DIM),
                                  den[:, g % 2, :, :].rearrange("p t (h a) -> p (t h) a", a=1)
                                  .broadcast_to([P, TT * 4, HEAD_DIM]), ALU.mult).then_inc(att_scaled, 1)

            def att_mix_lo(g):
                dve.wait_ge(att_hi, g + 1)
                dve.tensor_tensor(mix[:, 2 * g:2 * g + 2, SEQ:2 * SEQ],
                                  bank_ao[:, :].rearrange("p (a t) -> p a t", a=2),
                                  mix[:, 2 * g:2 * g + 2, 0:SEQ].bitcast(F32), ALU.subtract)\
                    .then_inc(att_lo, 1)

            def attention(g, quad):
                if g:
                    invert_sums(g - 1)
                make_lo(quad + 1, 0)
                dve.wait_ge(att_rs, g + 2)
                dve.scalar_tensor_tensor(QN[:, :, :].rearrange("p a t -> p (a t)"),
                                         bank[(quad - 1) % 2][:, :], q_gain[:, :],
                                         RS[:, :], ALU.mult, ALU.mult).then_inc(qk_normed, 1)
                bias_and_max(g, 0)
                if g:
                    scale_output(g - 1)
                make_lo(quad + 1, 1)
                bias_and_max(g, 1)
                bias_and_max(g, 2)
                if g:
                    att_mix_lo(g - 1)
                make_lo(quad + 1, 2)
                bias_and_max(g, 3)
                make_lo(quad + 1, 3)

            for g in range(Q_GROUPS):
                attention(g, g + 2)

            def clamp(n):
                dve.wait_ge(sg_exp, n + 1)
                dve.tensor_scalar(SG[:, :], SG[:, :], EXP_MAX, None, ALU.min).then_inc(sg_clamped, 1)

            def left_exponents(l):
                w = (LEVELS + [P])[l]
                b_left, _ = halves(B[:, :], w)
                r = b_left[:, :, w - 1:w].broadcast_to([P, SEQ // w, w])
                return dve.tensor_tensor(E[:, l, 0, :].rearrange("p (n w) -> p n w", w=w), r, b_left,
                                         ALU.subtract)

            def right_exponents(l):
                w = LEVELS[l]
                b_left, b_right = halves(B[:, :], w)
                r = b_left[:, :, w - 1:w].broadcast_to([P, SEQ // w, w])
                return dve.tensor_tensor(E[:, l, 1, :].rearrange("p (n w) -> p n w", w=w), b_right, r,
                                         ALU.subtract)

            def scale_k(l):
                w = LEVELS[l]
                k_left, _ = halves(K[:, :, :].rearrange("p a t -> p (a t)"), w)
                x_left, _ = halves(XK[:, l, :], w)
                return dve.tensor_tensor(x_left, k_left, E[:, l, 0, :].rearrange("p (n w) -> p n w", w=w),
                                         ALU.mult)

            def scale_q(l):
                w = (LEVELS + [P])[l]
                _, q_right = halves(QE[:, :, :].rearrange("p a t -> p (a t)"), w)
                e = E[:, l, 1, :].rearrange("p (n w) -> p n w", w=w)
                return dve.tensor_tensor(e, q_right, e, ALU.mult)

            def q_slot(j, quad, attention_ends=False):
                clamp(j * 3)
                if attention_ends:
                    invert_sums(Q_GROUPS - 1)
                make_lo(quad + 1, 0)
                dve.wait_ge(forget_scaled, j * 2 + 2)
                fe = FE[:, :, :].rearrange("p a t -> p (a t)")
                dve.tensor_scalar(fe, fe, FORGET_MIN, None, ALU.max).then_inc(forget_made, 1)
                dve.wait_ge(forget_made, j + 1)
                dve.tensor_scalar(K[:, :, :].rearrange("p a t -> p (a t)"), fe, -1.0, 1.0,
                                  ALU.mult, ALU.add).then_inc(k_made, 1)
                make_lo(quad + 1, 1)
                if attention_ends:
                    scale_output(Q_GROUPS - 1)
                    att_mix_lo(Q_GROUPS - 1)
                dve.wait_ge(log_made, j + 1)
                dve.tensor_tensor_scan(B[:, :], tile_start[:, :], LF[:, :], 0.0, ALU.mult, ALU.add)\
                    .then_inc(sum_made, 1)
                make_lo(quad + 1, 2)
                dve.wait_ge(sum_made, j + 1)
                for l in range(4):
                    left_exponents(l)
                    last = right_exponents(l)
                last.then_inc(exponents_made, 1)
                make_lo(quad + 1, 3)
                for l in range(4, NL):
                    left_exponents(l)
                    right_exponents(l)
                left_exponents(NL).then_inc(exponents_made, 1)

            def i_slot(j, quad):
                clamp(j * 3 + 1)
                dve.wait_ge(xk_cleared, 1)
                make_lo(quad + 1, 0)
                dve.wait_ge(decays_made, j * 2 + 1)
                for l in range(4):
                    scale_k(l)
                dve.wait_ge(sg_made, j * 3 + 2)
                q = QE[:, :, :].rearrange("p a t -> p (a t)")
                dve.tensor_tensor(q, bank_q[:, :], SG[:, :], ALU.mult).then_inc(silu_q, 1)
                make_lo(quad + 1, 1)
                dve.wait_ge(decays_made, j * 2 + 2)
                for l in range(4, NL):
                    scale_k(l)
                dve.tensor_tensor(E[:, NL, 0, :].rearrange("p (h t) -> p h t", h=2), K[:, :, 0:P],
                                  E[:, NL, 0, :].rearrange("p (h t) -> p h t", h=2), ALU.mult)
                make_lo(quad + 1, 2)
                dve.wait_ge(silu_q, j + 1)
                for l in range(NL + 1):
                    scale_q(l)
                dve.tensor_tensor(Q1[:, :], q[:, 1::2], FE[:, :, :].rearrange("p a t -> p (a t)")[:, 1::2],
                                  ALU.mult).then_inc(q_scaled, 1)
                make_lo(quad + 1, 3)

            def gather_scores(j, h):
                n = j * 2 + h
                dve.wait_ge(levels_made, n + 1)
                st = ST[:, h, 0:TT, :].rearrange("p t c -> p (t c)")
                banks = bank_scores[h]
                b, at = level_columns(NL - 1)
                _, st_right = halves(st, HALF)
                dve.tensor_copy(st_right, banks[b][:, at:at + P].rearrange("p (t c) -> p t c", t=TT))\
                    .then_inc(st_written, 1)
                dve.tensor_copy(ST[:, h, TT, :], banks[2][:, CROSS])
                for l, w in enumerate(MASKED_LEVELS):
                    b, at = level_columns(l if w > 1 else NL)
                    _, st_right = halves(st, w)
                    dve.wait_ge(st_written, n * (NL + 1) + l + 1)
                    dve.sem_inc(st_turn, 1)
                    dve.copy_predicated(
                        st_right,
                        level_mask[:, l, :, :].rearrange("p t c -> p (t c)").bitcast(I32)
                        .rearrange("p (n w) -> p n w", w=w),
                        banks[b][:, at:at + P].rearrange("p (n w) -> p n w", w=w)).then_inc(st_written, 1)
                dve.wait_ge(st_written, (n + 1) * (NL + 1))
                dve.sem_inc(st_turn, 1)
                dve.copy_predicated(st, same_mask[:, :, :].rearrange("p t c -> p (t c)").bitcast(I32),
                                    banks[2][:, SAME]).then_inc(st_made, 1)

            def g_slot(j, quad):
                make_lo(quad + 1, 0)
                make_lo(quad + 1, 1)
                gather_scores(j, 0)
                make_lo(quad + 1, 2)
                gather_scores(j, 1)
                make_lo(quad + 1, 3)

            def f_slot_of_next(j, quad):
                clamp(j * 3 + 2)
                make_lo(quad + 1, 0)
                dve.wait_ge(sg_made, j * 3 + 3)
                ge = GE[:, :, :].rearrange("p a t -> p (a t)")
                dve.tensor_tensor(ge, bank_g[:, :], SG[:, :], ALU.mult).then_inc(silu_g, 1)
                make_lo(quad + 1, 1)
                dve.wait_ge(o_rs, j + 1)
                dve.tensor_tensor(SQ[:, :], RS[:, :], bank_o[:, :], ALU.mult).then_inc(o_normed, 1)
                dve.wait_ge(o_normed, j + 1 + FREE)
                dve.scalar_tensor_tensor(RS[:, :], SQ[:, :], cols[:, HG_GAIN:HG_GAIN + 1], ge,
                                         ALU.mult, ALU.mult).then_inc(o_gated, 1)
                make_lo(quad + 1, 2)
                make_lo(quad + 1, 3)
                dve.wait_ge(hg_hi, j + 1)
                rows_of = bass.ds(j * 2 + KT // 2, 2)
                dve.tensor_tensor(mix[:, rows_of, SEQ:2 * SEQ],
                                  RS[:, :].rearrange("p (a t) -> p a t", a=2),
                                  mix[:, rows_of, 0:SEQ].bitcast(F32), ALU.subtract).then_inc(hg_lo, 1)

            q_slot(0, Q_F0 + 1, attention_ends=True)
            with dve.Fori(0, PAIRS - 1) as j:
                i_slot(j, j * 4 + Q_F0 + 2)
                g_slot(j, j * 4 + Q_F0 + 3)
                f_slot_of_next(j, j * 4 + Q_F0 + 4)
                q_slot(j + 1, j * 4 + Q_F0 + 5)
            i_slot(PAIRS - 1, Q_OUT - 2)
            g_slot(PAIRS - 1, Q_OUT - 1)
            f_slot_of_next(PAIRS - 1, Q_OUT)

            def add_to_x(group, units, n):
                dve.wait_ge(units_used, units + RING)
                c = bass.ds(n * GT, GT)
                for t in range(TT):
                    last = dve.tensor_tensor(xt[:, t, c], xt[:, t, c], pair_of(group)[t][:, :], ALU.add)
                last.then_inc(groups_evacuated, 1)

            def second_norm(n):
                for t in range(TT):
                    h_lo_round(1, n, t, (KT // 4 + n) * TT + t, bank[4 + t])

            for i in range(RING):
                make_lo(Q_OUT + 2, i)
            for n in range(1, OUT_GROUPS):
                add_to_x(G_OUT + n - 1, (Q_OUT + n * QUADS_OUT) * RING, n - 1)
                make_lo(Q_OUT + 2 * n + 1, 0)
                second_norm(n - 1)
                for i in range(1, RING):
                    make_lo(Q_OUT + 2 * n + 1, i)
                for i in range(RING):
                    make_lo(Q_OUT + 2 * n + 2, i)
            add_to_x(G_UP - 1, Q_UP * RING, OUT_GROUPS - 1)
            dve.memset(U[:, :, 0:2], 0.0).then_inc(u_cleared, 1)
            make_lo(Q_UP + 1, 0)
            second_norm(OUT_GROUPS - 1)
            dve.wait_ge(x_squared, TT + TT * OUT_GROUPS)
            dve.tensor_reduce(ss[:, :], ss_part[:, :, :], AX, ALU.add).then_inc(x_summed, 1)
            for i in range(1, RING):
                make_lo(Q_UP + 1, i)
            dve.wait_ge(row_made, 1)

            def taps(n, ab, g, quad):
                dst = U[:, :, 2:SEQ + 2]
                evacuate(G_UP + ab, n, (n + Q_UP + 1) * RING, dst)
                make_lo(quad, 0)
                for tap, before, after in ((1, tap2, tap1), (0, tap1, tap0)):
                    for c in range(2):
                        col = g * 2 + ab * (N_CONV // 2) + c + conv_col(tap)
                        dve.wait_ge(before, n * 2 + c + 1)
                        dve.scalar_tensor_tensor(C[:, ab, c, :], U[:, c, tap:tap + SEQ],
                                                 cols[:, bass.ds(col, 1)], C[:, ab, c, :],
                                                 ALU.mult, ALU.add).then_inc(after, 1)
                make_lo(quad, 1)

            def a_work(g, quad):
                taps(g * 2, 0, g, quad)
                for i in range(2, RING):
                    make_lo(quad, i)

            def b_work(g, quad):
                taps(g * 2 + 1, 1, g, quad)
                dve.wait_ge(silu_a, g + 1)
                dve.wait_ge(tap0, g * 4 + 4)
                a = C[:, 0, :, :].rearrange("p c t -> p (c t)")
                b = C[:, 1, :, :].rearrange("p c t -> p (c t)")
                dve.tensor_tensor(b, a, b, ALU.mult).then_inc(ab_made, 1)
                make_lo(quad, 2)
                dve.wait_ge(gated_hi, g + 1)
                dve.tensor_tensor(gated[:, bass.ds(g * 2, 2), SEQ:2 * SEQ], C[:, 1, :, :],
                                  gated[:, bass.ds(g * 2, 2), 0:SEQ].bitcast(F32), ALU.subtract)\
                    .then_inc(gated_lo, 1)
                make_lo(quad, 3)

            with dve.Fori(0, UP_GROUPS - 1) as g:
                a_work(g, g * 2 + Q_UP + 2)
                b_work(g, g * 2 + Q_UP + 3)
            a_work(UP_GROUPS - 1, Q_DOWN)
            b_work(UP_GROUPS - 1, Q_DOWN + 1)
            for n in range(OUT_GROUPS):
                for u in range(n * DOWN_UNITS, (n + 1) * DOWN_UNITS):
                    if u >= 2 * RING:
                        make_lo(Q_DOWN + u // RING, u % RING)
                    if n and u == n * DOWN_UNITS + RING - 1:
                        add_to_x(G_DOWN + n - 1, Q_DOWN * RING + n * DOWN_UNITS, n - 1)
            c = slice((OUT_GROUPS - 1) * GT, OUT_GROUPS * GT)
            for t in range(TT):
                if t == 0:
                    dve.wait_ge(first_tile_done, OUT_GROUPS)
                else:
                    dve.wait_ge(units_used, Q_DOWN * RING + OUT_GROUPS * DOWN_UNITS + RING)
                dve.tensor_tensor(xt[:, t, c], xt[:, t, c], pair_of(G_DOWN + OUT_GROUPS - 1)[t][:, :], ALU.add)\
                    .then_inc(last_added, 1)

        @block.tensor
        def _(pe):
            def transpose(dst, src, n=P):
                return pe.transpose(dst, src, ident[0:n, 0:n])

            def norm_round(n):
                k, t = NORM_ROUNDS[n]
                pe.wait_ge(x_scaled, t * KT // 4 + k + 1)
                if n >= 4:
                    pe.wait_ge(h_lo, n - 3)
                for i in range(4):
                    last = transpose(bank[4 + n % 4][:, i * P:(i + 1) * P],
                                     squares[:, t, (4 * k + i) * P:(4 * k + i + 1) * P])
                last.then_inc(x_transposed, 1)

            def second_norm(n):
                pe.wait_ge(groups_evacuated, G_OUT + n + 1 + BANK_PAIRS)
                if n:
                    pe.wait_ge(h_lo, (KT // 4 + n) * TT)
                for t in range(TT):
                    for i in range(4):
                        last = transpose(bank[4 + t][:, i * P:(i + 1) * P],
                                         xt[:, t, (4 * n + i) * P:(4 * n + i + 1) * P])
                    last.then_inc(x_transposed, 1)

            def unit_channels(quad, i, group):
                pe.wait_ge(units_split, quad * RING + i + 1 + RING)
                banks = pair_of(group)
                for k in range(4):
                    for b in range(2):
                        c = slice(k * GC + b * P, k * GC + (b + 1) * P)
                        x_k = hs[:, 4 * i + k, :]
                        pe.matmul(banks[b][:, :], w_hi[:, i, c], x_k, start=(i == 0 and k == 0), stop=False)
                        last = pe.matmul(banks[b][:, 0:SEQ], w_lo[:, i, c], x_k[:, 0:SEQ], start=False,
                                         stop=(i == RING - 1 and k == 3))
                last.then_inc(units_used, 1)

            def unit_w_in(quad, i, dst):
                pe.wait_ge(units_split, quad * RING + i + 1 + RING)
                for k in range(4):
                    x_hi, x_lo = hs[:, 4 * i + k, 0:SEQ], hs[:, 4 * i + k, SEQ:2 * SEQ]
                    for b in range(2):
                        c = slice(k * GC + b * P, k * GC + (b + 1) * P)
                        o = dst[:, b * SEQ:(b + 1) * SEQ]
                        pe.matmul(o, w_hi[:, i, c], x_hi, start=(i == 0 and k == 0 and b == 0), stop=False,
                                  skip_group_check=True)
                        pe.matmul(o, w_hi[:, i, c], x_lo, start=False, stop=False, skip_group_check=True)
                        last = pe.matmul(o, w_lo[:, i, c], x_hi, start=False,
                                         stop=(i == RING - 1 and k == 3), skip_group_check=True)
                last.then_inc(units_used, 1)

            def unit_tokens(quad, i, group, src, k0, k_all, signal_first_tile=False):
                pe.wait_ge(units_split, quad * RING + i + 1 + RING)
                banks = pair_of(group)
                for t in range(TT):
                    for k in range(2):
                        hi, lo = w_hi[:, i, k * GT:(k + 1) * GT], w_lo[:, i, k * GT:(k + 1) * GT]
                        x_hi = src[:, k0 + k, t * P:(t + 1) * P]
                        x_lo = src[:, k0 + k, SEQ + t * P:SEQ + (t + 1) * P]
                        pe.matmul(banks[t][:, :], x_hi, hi, start=(k0 + k == 0), stop=False)
                        pe.matmul(banks[t][:, :], x_hi, lo, start=False, stop=False)
                        last = pe.matmul(banks[t][:, :], x_lo, hi, start=False, stop=(k0 + k == k_all - 1))
                    if t == 0 and signal_first_tile:
                        last.then_inc(first_tile_done, 1)
                last.then_inc(units_used, 1)

            pe.wait_ge(pool_done, 1)
            norm_round(0)
            pe.wait_ge(small_loaded, 16 * (2 + 1 + 4 + 1))
            transpose(bank[3][:, 0:N_SMALL], rows[0:N_SMALL, 0, :], N_SMALL).then_inc(rows_transposed, 1)
            for n in range(1, 7):
                norm_round(n)
            for i in range(RING):
                pe.wait_ge(h_lo, NORM_ROUNDS_OF_UNIT[i])
                unit_w_in(0, i, bank[0])
                if i == 0:
                    norm_round(7)
                    pe.wait_ge(conv_loaded, 16 * (1 + CONV + 1))
                    pe.wait_ge(cols_made, 1)
                    for c in range(1 + CONV):
                        at = N_SMALL + c * N_CONV
                        last = transpose(bank[3][:, at:at + N_CONV], rows[0:N_CONV, 1 + c, :], N_CONV)
                    last.then_inc(rows_transposed, 1)
            unit_w_in(1, 0, bank[1])
            pe.wait_ge(att_squared, 1)
            pe.matmul(bank[7][:, 0:SEQ], head_mean[:, :], SQ[:, 0:SEQ], start=True, stop=True)\
                .then_inc(att_mean, 1)
            pe.wait_ge(v_copied, 1)
            transpose(bank_p[0][:, 0:P], FE[:, 1, 0:P])
            transpose(bank_p[0][:, P:2 * P], FE[:, 1, CHUNK:P + CHUNK])
            transpose(bank_p[0][0:CHUNK, 2 * P:3 * P], FE[:, 1, P + CHUNK:SEQ]).then_inc(v_transposed, 1)
            for i in range(1, RING):
                unit_w_in(1, i, bank[1])

            def scores(g, h):
                a, half = divmod(h, 2)
                n = g * 4 + h
                k = kz[:, g // (Q_GROUPS // KV_HEADS) * 2 + half, :]
                out_b = bank_s[h % 2]
                if n >= 2:
                    pe.wait_ge(biased, n - 1)
                pe.matmul(out_b[:, 0:P], QN[:, a, 0:P], k[:, 0:P], start=True, stop=True)
                pe.matmul(out_b[:, P:KEYS], QN[:, a, P:2 * P], k[:, CHUNK:SEQ], start=True, stop=True)\
                    .then_inc(scores_made, 1)

            def turn_p(g, h):
                n = g * 4 + h
                out_b = bank_p[h % 2]
                pe.wait_ge(exp_made, n + 1)
                if n >= 2:
                    pe.wait_ge(pt_made, n - 1)
                transpose(out_b[:, 0:P], PR[:, h, 0:P])
                transpose(out_b[:, P:2 * P], PR[:, h, P:2 * P])
                transpose(out_b[0:CHUNK, 2 * P:3 * P], PR[:, h, 2 * P:KEYS]).then_inc(p_transposed, 1)

            def times_v(g, h):
                n = g * 4 + h
                if g and h == 0:
                    pe.wait_ge(att_scaled, g)
                pe.wait_ge(pt_made, n + 1)
                kv = g // (Q_GROUPS // KV_HEADS)
                c = slice(kv * HEAD_DIM, (kv + 1) * HEAD_DIM)
                o = [bank_pv[:, (t * 4 + h) * HEAD_DIM:(t * 4 + h + 1) * HEAD_DIM] for t in range(TT)]
                pt = PT[:, h % 2, :]
                pe.matmul(o[0], pt[:, 0:P], vt[:, 0, c], start=True, stop=True)
                pe.matmul(o[1], pt[:, P:2 * P], vt[:, 1, c], start=True, stop=False)
                pe.matmul(o[1], pt[0:CHUNK, 2 * P:3 * P], vt[0:CHUNK, 2, c], start=False, stop=True)\
                    .then_inc(pv_made, 1)

            def turn_output(g):
                pe.wait_ge(att_scaled, g + 1)
                for a in range(2):
                    for t in range(TT):
                        last = transpose(bank_ao[:, (a * TT + t) * P:(a * TT + t + 1) * P],
                                         AO[:, t, a * P:(a + 1) * P])
                last.then_inc(att_transposed, 1)

            def attention(g, quad):
                dst = bank[quad % 2]
                pe.wait_ge(qk_normed, g + 1)
                unit_w_in(quad, 0, dst)
                if g:
                    turn_p(g - 1, 3)
                    times_v(g - 1, 2)
                if g > 1:
                    pe.wait_ge(att_lo, g - 1)
                pe.wait_ge(att_squared, g + 2)
                pe.matmul(bank_m[:, :], head_mean[:, :], SQ[:, :], start=True, stop=True)\
                    .then_inc(att_mean, 1)
                unit_w_in(quad, 1, dst)
                if g:
                    times_v(g - 1, 3)
                pe.wait_ge(qk_normed, g + 2)
                pe.wait_ge(kz_made, 6)
                scores(g, 0)
                scores(g, 1)
                unit_w_in(quad, 2, dst)
                if g:
                    turn_output(g - 1)
                pe.wait_ge(vt_made, 1)
                turn_p(g, 0)
                scores(g, 2)
                scores(g, 3)
                unit_w_in(quad, 3, dst)
                turn_p(g, 1)
                times_v(g, 0)
                turn_p(g, 2)
                times_v(g, 1)

            for g in range(Q_GROUPS):
                attention(g, g + 2)

            def q_slot(quad):
                for i in range(RING):
                    unit_w_in(quad, i, bank_q)

            def i_slot(j, quad):
                pe.wait_ge(sg_exp, j * 3 + 1)
                for i in range(RING):
                    unit_w_in(quad, i, bank_i)

            def head_scores(h):
                banks = bank_scores[h]
                for t in range(TT):
                    c = slice(h * SEQ + t * P, h * SEQ + (t + 1) * P)
                    right = slice((h * TT + t) * HALF, (h * TT + t + 1) * HALF)
                    k = K[:, h, t * P:(t + 1) * P]
                    for l in range(NL + 1):
                        b, at = level_columns(l)
                        at += t * HALF
                        pe.matmul(banks[b][:, at:at + HALF], XK[:, l, c] if l < NL else k,
                                  E[:, l, 1, right] if l < NL else Q1[:, right], start=True, stop=True)
                    pe.matmul(banks[2][:, t * P:(t + 1) * P], k, QE[:, h, t * P:(t + 1) * P],
                              start=True, stop=True)
                tile = slice(h * P, (h + 1) * P)
                pe.matmul(banks[2][:, CROSS], E[:, NL, 0, tile], E[:, NL, 1, tile], start=True, stop=True)\
                    .then_inc(levels_made, 1)

            def g_slot(j, quad):
                pe.wait_ge(silu_q, j + 1)
                unit_w_in(quad, 0, bank_g)
                pe.wait_ge(o_normed, j + FREE)
                pe.wait_ge(i_copied, j + 1)
                for h in range(2):
                    for t in range(TT):
                        last = transpose(bank_v[:, (h * TT + t) * P:(h * TT + t + 1) * P],
                                         IE[:, h, t * P:(t + 1) * P])
                last.then_inc(i_transposed, 1)
                unit_w_in(quad, 1, bank_g)
                pe.wait_ge(q_scaled, j + 1)
                head_scores(0)
                unit_w_in(quad, 2, bank_g)
                pe.wait_ge(v_made, j + 1)
                head_scores(1)
                unit_w_in(quad, 3, bank_g)

            def output(j):
                pe.wait_ge(st_made, j * 2 + 2 + FREE)
                for h in range(2):
                    o = h * SEQ
                    pe.matmul(bank_o[:, o:o + P], V[:, h, 0, :], ST[:, h, 0, :], start=True, stop=True)
                    pe.matmul(bank_o[:, o + P:o + SEQ], V[:, h, 0, :], ST[:, h, 2, :], start=True, stop=False)
                    last = pe.matmul(bank_o[:, o + P:o + SEQ], V[:, h, 1, :], ST[:, h, 1, :],
                                     start=False, stop=True)
                last.then_inc(o_made, 1)

            def output_mean(j):
                pe.wait_ge(o_squared, j + 1)
                pe.matmul(bank_mean[:, :], all_mean[:, :], SQ[:, :], start=True, stop=True)\
                    .then_inc(o_mean, 1)

            def f_slot_of_next(j, quad):
                unit_w_in(quad, 0, bank_f)
                output(j)
                unit_w_in(quad, 1, bank_f)
                output_mean(j)
                unit_w_in(quad, 2, bank_f)
                unit_w_in(quad, 3, bank_f)

            pe.wait_ge(qk_normed, 1 + Q_GROUPS)
            unit_w_in(Q_F0 + 1, 0, bank_q)
            turn_p(Q_GROUPS - 1, 3)
            times_v(Q_GROUPS - 1, 2)
            unit_w_in(Q_F0 + 1, 1, bank_q)
            times_v(Q_GROUPS - 1, 3)
            unit_w_in(Q_F0 + 1, 2, bank_q)
            turn_output(Q_GROUPS - 1)
            unit_w_in(Q_F0 + 1, 3, bank_q)
            with pe.Fori(0, PAIRS - 1) as j:
                i_slot(j, j * 4 + Q_F0 + 2)
                g_slot(j, j * 4 + Q_F0 + 3)
                f_slot_of_next(j, j * 4 + Q_F0 + 4)
                pe.wait_ge(silu_g, j + 1)
                q_slot(j * 4 + Q_F0 + 5)
            i_slot(PAIRS - 1, Q_OUT - 2)
            g_slot(PAIRS - 1, Q_OUT - 1)

            pe.wait_ge(att_lo, Q_GROUPS)
            pe.wait_ge(st_made, 2 * PAIRS - 1 + FREE)
            for n in range(OUT_GROUPS):
                pe.wait_ge(groups_evacuated, G_OUT + n + 1)
                for u in range(KT // 2):
                    if n == 0 and 2 * u >= KT // 2:
                        pe.wait_ge(hg_lo, u - KT // 4 + 1)
                    unit_tokens(Q_OUT + n * QUADS_OUT + u // RING, u % RING, G_OUT + n, mix, 2 * u, KT)
                    if n == 0 and u == 0:
                        output(PAIRS - 1)
                    if n == 0 and u == 1:
                        output_mean(PAIRS - 1)
                    if n and u == 1:
                        second_norm(n - 1)

            pe.wait_ge(groups_evacuated, G_UP + 1)
            for i in range(RING):
                pe.wait_ge(h_lo, (KT // 4 + i + 1) * TT)
                unit_channels(Q_UP, i, G_UP)
                if i == 1:
                    second_norm(OUT_GROUPS - 1)
            pe.wait_ge(groups_evacuated, G_UP + 2)
            for i in range(RING):
                unit_channels(Q_UP + 1, i, G_UP + 1)
                if i == 0:
                    pe.wait_ge(x_diag, TT)
                    pe.matmul(bank[6][:, 0:SEQ], all_mean[:, :],
                              rms_diag[:, :, :].rearrange("p t c -> p (t c)"),
                              start=True, stop=True).then_inc(row_spread, 1)
            with pe.Fori(1, UP_GROUPS) as g:
                for ab in range(2):
                    pe.wait_ge(groups_evacuated, g * 2 + ab + G_UP + 1)
                    for i in range(RING):
                        unit_channels(g * 2 + ab + Q_UP, i, G_UP + ab)

            with pe.Fori(0, OUT_GROUPS // 2) as m:
                for v in range(2 * DOWN_UNITS):
                    n, u = divmod(v, DOWN_UNITS)
                    if u == 0:
                        pe.wait_ge(groups_evacuated, m * 2 + n + G_DOWN + 1)
                    if v == DOWN_UNITS - 1:
                        pe.wait_ge(gated_lo, UP_GROUPS)
                    unit_tokens(m * (2 * DOWN_UNITS // RING) + Q_DOWN + v // RING, v % RING,
                                G_DOWN + n, gated, 2 * u, KT_FF, signal_first_tile=(u == DOWN_UNITS - 1))


_INS = ["x", "attn_norm", "w_in", "q_norm", "k_norm", "attn_sinks", "hg_lb_logits", "hg_norm", "w_out",
        "ffn_norm", "w_ffn_up", "ffn_conv_w", "ffn_conv_b", "w_ffn_down"]
_LAYER = {"w_in", "w_out", "w_ffn_up", "ffn_conv_w", "w_ffn_down"}


def kernel(**inputs):
    import numpy as _np
    import concourse.bacc as _bacc
    from concourse import mybir as _mybir
    from concourse.bass_utils import run_bass_kernel_spmd as _run

    nc = _bacc.Bacc("TRN2", target_bir_lowering=False, num_devices=1)
    arrays, args = {}, []
    for name in _INS:
        a = _np.ascontiguousarray(inputs[name])
        if name in _LAYER or name == "x":
            a = a[0]
        arrays[f"in_{name}_dram"] = a
        args.append(nc.dram_tensor(f"in_{name}_dram", a.shape, _mybir.dt.from_np(a.dtype),
                                   kind="ExternalInput").ap())
    out = nc.dram_tensor("out_dram", (SEQ, D_MODEL), _mybir.dt.float32, kind="ExternalOutput").ap()
    hybrid_layer(nc, *args, out)
    r = _run(nc, [arrays], core_ids=[0])
    return r.results[0]["out_dram"].reshape(1, SEQ, D_MODEL)
```
